# Optimizing a Trainium2 kernel written in Bass

```python
import jax
import jax.numpy as jnp
from jax import lax
import numpy as np

D_MODEL = 1024
BATCH = 1
SEQ = 2048
DEPTH = 1

CHUNK = 64
N_META = 16
HEAD_DIM = 64
N_Q_HEADS = 16
N_KV_HEADS = 2
Q_PER_KV = N_Q_HEADS // N_KV_HEADS
ATTN_WIDTH = N_Q_HEADS * HEAD_DIM
KV_WIDTH = N_KV_HEADS * HEAD_DIM
WINDOW = 128
WINDOW_CHUNKS = WINDOW // CHUNK
ROT_DIM = HEAD_DIM // 4
ROPE_THETA = 500000.0
POOL_WINDOWS = (2, 4, 8, 16)
N_POOL_GROUPS = len(POOL_WINDOWS)
POOL_WIDTH = D_MODEL
POOL_GROUP_DIM = POOL_WIDTH // N_POOL_GROUPS
MIX_WIDTH = ATTN_WIDTH + POOL_WIDTH
SPLIT_SIZES = (ATTN_WIDTH, KV_WIDTH, KV_WIDTH, ATTN_WIDTH, POOL_WIDTH, POOL_WIDTH)
IN_WIDTH = sum(SPLIT_SIZES)
SPLIT_POINTS = tuple(int(s) for s in np.cumsum(SPLIT_SIZES)[:-1])
EPS = 1e-6
NEG_INF = -1e30

kernel_name = "hymba_swa_sink_pool_hybrid"

def rms_norm(x, gain):
    xf = x.astype(jnp.float32)
    y = xf * lax.rsqrt(jnp.mean(xf * xf, axis=-1, keepdims=True) + EPS)
    return (y * gain.astype(jnp.float32)).astype(x.dtype)

def partial_rotary(x, pos):
    half = ROT_DIM // 2
    inv_freq = ROPE_THETA ** (-jnp.arange(half, dtype=jnp.float32) * (2.0 / ROT_DIM))
    ang = pos.astype(jnp.float32)[:, None] * inv_freq[None, :]
    cos = jnp.cos(ang)[None, :, None, :]
    sin = jnp.sin(ang)[None, :, None, :]
    xr = x[..., :ROT_DIM].astype(jnp.float32)
    x1, x2 = xr[..., :half], xr[..., half:]
    rot = jnp.concatenate([x1 * cos - x2 * sin, x2 * cos + x1 * sin], axis=-1)
    return jnp.concatenate([rot.astype(x.dtype), x[..., ROT_DIM:]], axis=-1)

def sink_attention(q, k, v, valid, sinks):
    s = jnp.einsum("bnqhgd,bnkhd->bnhgqk", q, k, preferred_element_type=jnp.float32)
    s = s.astype(jnp.float32) * (HEAD_DIM ** -0.5)
    s = jnp.where(valid[None, :, None, None, None, :], s, NEG_INF)
    sink = sinks.astype(jnp.float32).reshape(N_KV_HEADS, Q_PER_KV)[None, None, :, :, None, None]
    m = jnp.maximum(jnp.max(s, axis=-1, keepdims=True), sink)
    p = jnp.exp(s - m)
    denom = jnp.sum(p, axis=-1, keepdims=True) + jnp.exp(sink - m)
    p = (p / denom).astype(v.dtype)
    return jnp.einsum("bnhgqk,bnkhd->bnqhgd", p, v)

def chunked_window_attention(q, k, v, sinks):
    b, L = q.shape[0], q.shape[1]
    n_chunks = (L - N_META) // CHUNK
    q = q.reshape(b, L, N_KV_HEADS, Q_PER_KV, HEAD_DIM)
    q_meta, q_real = q[:, :N_META], q[:, N_META:]
    k_meta, k_real = k[:, :N_META], k[:, N_META:]
    v_meta, v_real = v[:, :N_META], v[:, N_META:]
    o_meta = sink_attention(q_meta[:, None], k_meta[:, None], v_meta[:, None],
                            jnp.ones((1, N_META), dtype=bool), sinks)[:, 0]
    q_c = q_real.reshape(b, n_chunks, CHUNK, N_KV_HEADS, Q_PER_KV, HEAD_DIM)
    k_c = k_real.reshape(b, n_chunks, CHUNK, N_KV_HEADS, HEAD_DIM)
    v_c = v_real.reshape(b, n_chunks, CHUNK, N_KV_HEADS, HEAD_DIM)
    chunk_idx = jnp.arange(n_chunks)
    meta_shape = (b, n_chunks, N_META, N_KV_HEADS, HEAD_DIM)
    k_parts = [jnp.broadcast_to(k_meta[:, None], meta_shape)]
    v_parts = [jnp.broadcast_to(v_meta[:, None], meta_shape)]
    valid_parts = [jnp.ones((n_chunks, N_META), dtype=bool)]
    for shift in range(WINDOW_CHUNKS - 1, -1, -1):
        pad = ((0, 0), (shift, 0), (0, 0), (0, 0), (0, 0))
        k_parts.append(jnp.pad(k_c, pad)[:, :n_chunks])
        v_parts.append(jnp.pad(v_c, pad)[:, :n_chunks])
        valid_parts.append(jnp.broadcast_to((chunk_idx >= shift)[:, None], (n_chunks, CHUNK)))
    k_win = jnp.concatenate(k_parts, axis=2)
    v_win = jnp.concatenate(v_parts, axis=2)
    valid = jnp.concatenate(valid_parts, axis=1)
    o_real = sink_attention(q_c, k_win, v_win, valid, sinks)
    o_real = o_real.reshape(b, n_chunks * CHUNK, N_KV_HEADS, Q_PER_KV, HEAD_DIM)
    o = jnp.concatenate([o_meta, o_real], axis=1)
    return o.reshape(b, L, ATTN_WIDTH)

def multiscale_pool_mixer(u, w_pool, pool_scale):
    b, L = u.shape[0], u.shape[1]
    uf = u.astype(jnp.float32).reshape(b, L, N_POOL_GROUPS, POOL_GROUP_DIM)
    cs = jnp.pad(jnp.cumsum(uf, axis=1), ((0, 0), (1, 0), (0, 0), (0, 0)))
    t = jnp.arange(L)
    means = []
    for g, w in enumerate(POOL_WINDOWS):
        lo = jnp.maximum(t + 1 - w, 0)
        csg = cs[:, :, g]
        win_sum = csg[:, 1:] - csg[:, lo]
        count = (t + 1 - lo).astype(jnp.float32)[None, :, None]
        means.append(win_sum / count)
    pooled = jnp.stack(means, axis=2) - uf
    mixed = jnp.einsum("blgc,gcd->blgd", pooled, w_pool.astype(jnp.float32))
    return (mixed.reshape(b, L, POOL_WIDTH) * pool_scale.astype(jnp.float32)).astype(u.dtype)

def setup_inputs(seed: int = 0) -> dict:
    key = jax.random.key(seed)
    ks = jax.random.split(key, 9)
    f32 = jnp.float32
    x = jax.random.normal(ks[0], (BATCH, SEQ, D_MODEL), f32)
    meta_tokens = jax.random.normal(ks[1], (N_META, D_MODEL), f32)
    norm_gain = 1.0 + 0.02 * jax.random.normal(ks[2], (DEPTH, D_MODEL), f32)
    w_in = jax.random.normal(ks[3], (DEPTH, D_MODEL, IN_WIDTH), f32) * (D_MODEL ** -0.5)
    attn_sinks = jax.random.normal(ks[4], (DEPTH, N_Q_HEADS), f32)
    w_pool = jax.random.normal(ks[5], (DEPTH, N_POOL_GROUPS, POOL_GROUP_DIM, POOL_GROUP_DIM), f32) * (POOL_GROUP_DIM ** -0.5)
    pool_scale = 1.0 + 0.1 * jax.random.normal(ks[6], (DEPTH, POOL_WIDTH), f32)
    w_out = jax.random.normal(ks[7], (DEPTH, MIX_WIDTH, D_MODEL), f32) * (MIX_WIDTH ** -0.5)
    final_norm_gain = 1.0 + 0.02 * jax.random.normal(ks[8], (D_MODEL,), f32)
    return {"x": x, "meta_tokens": meta_tokens, "norm_gain": norm_gain, "w_in": w_in,
            "attn_sinks": attn_sinks, "w_pool": w_pool, "pool_scale": pool_scale,
            "w_out": w_out, "final_norm_gain": final_norm_gain}

def reference(x, meta_tokens, norm_gain, w_in, attn_sinks, w_pool, pool_scale, w_out, final_norm_gain):
    b = x.shape[0]
    meta = jnp.broadcast_to(meta_tokens[None].astype(x.dtype), (b, N_META, D_MODEL))
    h = jnp.concatenate([meta, x], axis=1)
    L = h.shape[1]
    pos = jnp.arange(L, dtype=jnp.int32)
    for layer in range(DEPTH):
        z = rms_norm(h, norm_gain[layer])
        proj = jnp.einsum("bld,de->ble", z, w_in[layer])
        q, k, v, g_attn, u_pool, g_pool = jnp.split(proj, SPLIT_POINTS, axis=-1)
        q = partial_rotary(q.reshape(b, L, N_Q_HEADS, HEAD_DIM), pos)
        k = partial_rotary(k.reshape(b, L, N_KV_HEADS, HEAD_DIM), pos)
        v = v.reshape(b, L, N_KV_HEADS, HEAD_DIM)
        o_attn = chunked_window_attention(q, k, v, attn_sinks[layer])
        o_pool = multiscale_pool_mixer(u_pool, w_pool[layer], pool_scale[layer])
        gated = jnp.concatenate([jax.nn.silu(g_attn) * o_attn, jax.nn.silu(g_pool) * o_pool], axis=-1)
        h = h + jnp.einsum("ble,ed->bld", gated, w_out[layer])
    return rms_norm(h, final_norm_gain)[:, N_META:]


_drawn_inputs = setup_inputs


def setup_inputs(seed=0):
    import zlib

    import numpy as np

    out = dict(_drawn_inputs(seed))
    spreads = {}
    factors = {'meta_tokens': 2.77, 'norm_gain': 5.472, 'attn_sinks': 8.0, 'final_norm_gain': 2.996}
    for name, (base, spread) in spreads.items():
        noise = np.random.default_rng([zlib.crc32(name.encode()), seed]).standard_normal(out[name].shape)
        drawn = base * np.exp(spread * noise) if base else spread * noise
        out[name] = jnp.asarray(drawn.astype(out[name].dtype))
    for name, factor in factors.items():
        out[name] = (out[name] * factor).astype(out[name].dtype)
    return out
```

```python
from contextlib import ExitStack

import numpy as np

import concourse.bass as bass
from concourse import mybir

F32 = mybir.dt.float32
F32R = mybir.dt.float32r
ACT = mybir.ActivationFunctionType
ALU = mybir.AluOpType
AXX = mybir.AxisListType.X

P = 128
D = 1024
KT = D // P
SEQ = 2048
META = 16
CH = 64
HD = 64
HALVES = 2
TOK = SEQ // HALVES
NTT = TOK // P
NCH = TOK // CH
TB = 512
NTB = TOK // TB
HT = 8
PT = 8
NG = 4
KEYS = META + 2 * CH
KPITCH = KEYS + META
META0 = 2 * CH
EPS = 1e-6
SCALE = HD ** -0.5
PRE = 32

A_TILES = 2 + 2 * HT
GROUP_BLOCKS = 6
B_BLOCKS = NG * GROUP_BLOCKS
C_STEPS = HT + PT
MZ = 1
TG = 2
TPG = NTT // TG
C_BLOCKS = TG * C_STEPS
BLOCKS = A_TILES + B_BLOCKS + C_BLOCKS
USES = A_TILES + B_BLOCKS
FREES = HT + 4 * NG


def build(nc, x, meta, wa, wb, wp, wo, gain_n, gain_f, consts, ident_d, rot, rot_meta, out):
    ctx = ExitStack()
    with ctx:
        base = 16512
        arena = ctx.enter_context(nc.sbuf_tensor("arena", [P, (229344 - base - 64) // 4], F32))
        cursor = [base]

        def at(offset, name, shape, dt=F32):
            return nc.alloc_sbuf_tensor_at(name, shape, dt, offset=offset)

        def place(name, shape, dt=F32):
            size = 4 * int(np.prod(shape[1:]))
            offset = cursor[0]
            cursor[0] += (size + 31) // 32 * 32
            return at(offset, name, shape, dt), offset

        zh, zh_at = place("zh", [P, NTT, KT, P], F32R)
        zl, _ = place("zl", [P, NTT, KT, P], F32R)
        hbuf = at(zh_at, "hbuf", [P, NTT, D])
        gates, g_at = place("gates", [P, HT, TOK])
        qk, qk_at = place("qk", [P, NCH, 1 + HT, CH])
        gates = at(g_at, "gates_all", [P, HT + PT, TOK])
        wraw, _ = place("wraw", [P, 1024])
        wh, _ = place("wh", [P, 2, 1024], F32R)
        wl, _ = place("wl", [P, 2, 1024], F32R)
        plh, pool_at = place("plh", [P, 2, TOK], F32R)
        pll, _ = place("pll", [P, 2, TOK], F32R)
        cos_t = at(pool_at, "cos_t", [P, TOK])
        sin_t = at(pool_at + 4096, "sin_t", [P, TOK])
        gsh = at(pool_at, "gsh", [P, 2, TB], F32R)
        gsl = at(pool_at + 4096, "gsl", [P, 2, TB], F32R)
        gainn = at(pool_at + 8192, "gainn", [P, D])
        swapped = at(pool_at + 12288, "swapped", [P, TOK])
        r_at = cursor[0]
        pth, pth_at = place("pth", [P, 2, TB], F32R)
        ptl, _ = place("ptl", [P, 2, TB], F32R)
        probs = at(pth_at, "probs", [P, 4, 2 * KEYS])
        ptm, _ = place("ptm", [P, TB], F32R)
        qh, _ = place("qh", [P, HT * CH], F32R)
        ql, _ = place("ql", [P, HT * CH], F32R)
        kmask, _ = place("kmask", [P, 2, CH])
        xr = at(r_at, "xr", [P, 4, D])
        cursor[0] = r_at + 4 * 4096
        ubuf, u_at = place("ubuf", [P, PRE + TOK])
        rotsrc = at(u_at, "rotsrc", [P, TOK])
        gainf = at(u_at, "gainf", [P, D])
        wsum, _ = place("wsum", [P, META + TOK])
        vtok, _ = place("vtok", [P, NTT, P])
        kh, _ = place("kh", [P, 2, KPITCH], F32R)
        kl, _ = place("kl", [P, 2, KPITCH], F32R)
        vh, _ = place("vh", [P, 4, HD], F32R)
        vl, _ = place("vl", [P, 4, HD], F32R)
        vmeta, _ = place("vmeta", [P, P], F32R)
        ident, _ = place("ident", [P, P])
        halo, _ = place("halo", [P, PT, META])
        zmh, _ = place("zmh", [P, KT, META], F32R)
        zml, _ = place("zml", [P, KT, META], F32R)
        cst, _ = place("cst", [P, 32])
        rotm, _ = place("rotm", [P, 2, META])
        km, _ = place("km", [P, META])
        kms, _ = place("kms", [P, META])
        kmm, _ = place("kmm", [P, 2, META])
        vm, _ = place("vm", [P, META])
        vmm, _ = place("vmm", [P, 2 * META])
        stat, _ = place("stat", [P, 72])
        small, _ = place("small", [P, 16])
        assert cursor[0] <= 229344, cursor[0]
        kvmask, invw, negfirst = cst[:, 0:2], cst[:, 2:6], cst[:, 6:10]
        sinks, pscale = cst[:, 10:18], cst[:, 18:26]
        mx, negm, sarg, esink = (stat[:, 8 * i:8 * i + 8] for i in range(4))
        den, dsum, rden, pgate = (stat[:, 8 * i:8 * i + 8] for i in range(4, 8))
        ssq, std, rstd = small[:, 0:4], small[:, 4:8], small[:, 8:12]
        epst = small[:, 12:13]
        nsinks = stat[:, 64:72]

        ps = ctx.enter_context(nc.psum_tensor("ps", [P, 8, TB], F32))
        OB, SPARE, PB = 4, 5, (6, 7)

        def sem(name):
            return ctx.enter_context(nc.semaphore(name))

        const_in = sem("const_in")
        meta_in = sem("meta_in")
        gn_in = sem("gn_in")
        gf_in = sem("gf_in")
        rot_tab = sem("rot_tab")
        x_in = [sem(f"x_in{i}") for i in range(4)]
        res_in = sem("res_in")
        w_in = sem("w_in")
        out_done = sem("out_done")
        z_ssq, z_std, z_rstd, z_norm, z_t, z_hi, z_lo = (sem("z_" + n) for n in ("ssq", "std", "rstd", "norm", "t", "hi", "lo"))
        w_hi, w_lo, c_used = sem("w_hi"), sem("w_lo"), sem("c_used")
        pb_done = [sem(f"pb_done{i}") for i in range(2)]
        pb_free = [sem(f"pb_free{i}") for i in range(2)]
        rot_in, rot_sw, rot_mul, rot_done = sem("rot_in"), sem("rot_sw"), sem("rot_mul"), sem("rot_done")
        v_in, v_t, v_tok = sem("v_in"), sem("v_t"), sem("v_tok")
        vmm_r, vm_t, vm_hi, vm_done = sem("vmm_r"), sem("vm_t"), sem("vm_hi"), sem("vm_done")
        m_done, m_ev = sem("m_done"), sem("m_ev")
        km_sw, km_chain, km_done = sem("km_sw"), sem("km_chain"), sem("km_done")
        tanh_r = sem("tanh_r")
        s_done, s_mask, s_max, s_negm, s_sarg, s_exp = (sem("s_" + n) for n in ("done", "mask", "max", "negm", "sarg", "exp"))
        d_sum, d_rcp, p_ready, t_done = sem("d_sum"), sem("d_rcp"), sem("p_ready"), sem("t_done")
        pt_hi, pt_lo = sem("pt_hi"), sem("pt_lo")
        o_done, o_gate = sem("o_done"), sem("o_gate")
        qs_hi, qs_lo, ks_m, ks_hi, qs_ready = sem("qs_hi"), sem("qs_lo"), sem("ks_m"), sem("ks_hi"), sem("qs_ready")
        vw_hi, vw_lo = sem("vw_hi"), sem("vw_lo")
        u_in, u_sum, u_pool, u_hi, u_lo, u_halo = (sem("u_" + n) for n in ("in", "sum", "pool", "hi", "lo", "halo"))
        gs_hi, gs_lo = sem("gs_hi"), sem("gs_lo")
        c_done, h_add = sem("c_done"), sem("h_add")
        f_ssq, f_std, f_rstd, f_out = sem("f_ssq"), sem("f_std"), sem("f_rstd"), sem("f_out")
        zero_r = sem("zero_r")
        eps_r = sem("eps_r")
        psc_r = sem("psc_r")

        def block_a(h, a):
            return BLOCKS * h + a

        def block_b(h, g, r):
            return BLOCKS * h + A_TILES + GROUP_BLOCKS * g + r

        def block_c(h, tg, e):
            return BLOCKS * h + A_TILES + B_BLOCKS + C_STEPS * tg + e

        def use_a(h, a):
            return USES * h + a

        def use_b(h, g, r):
            return USES * h + A_TILES + GROUP_BLOCKS * g + r

        LAST_BLOCK = BLOCKS * HALVES - 1
        CREDIT = 1

        def settle(eng):
            eng.wait_ge(const_in, 48)

        def slot_free(eng, h, pos):
            if not isinstance(pos, int) or pos >= 2:
                eng.wait_ge(pb_done[1], USES * h + pos - 1)
            elif h > 0:
                slot_free_c(eng, h - 1, TG, pos)

        def slot_free_c(eng, h, tg, e):
            if not isinstance(e, int) or e >= 2:
                eng.wait_ge(c_used, (TG * h + tg) * (C_STEPS - 1) + e - 1)
            elif tg == 0:
                eng.wait_ge(pb_done[1], USES * (h + 1) + e - 1)
            elif e == 0:
                eng.wait_ge(c_used, (TG * h + tg) * (C_STEPS - 1))
            else:
                eng.wait_ge(c_done, (TG * h + tg) * 2 * TPG)

        SMALL = 256

        def size_b(r):
            return SMALL if r >= 4 else 1024

        block = ctx.enter_context(nc.Block())

        @block.sync
        def _(sp):
            def load(b, src, size=1024, slot_first=False):
                if not slot_first:
                    sp.wait_ge(w_lo, b)
                sp.dma_start(wraw[:, 0:size], src).then_inc(w_in, 16)

            for h in range(HALVES):
                load(block_a(h, 0), wa[0], slot_first=h == 0)
                with sp.Fori(1, A_TILES) as a:
                    load(block_a(h, a), wa[a])
                with sp.Fori(0, NG) as g:
                    for r in range(4):
                        load(block_b(h, g, r), wb[g, r])
                    for r in range(2):
                        load(block_b(h, g, 4 + r), wp[g, r], SMALL)
                for tg in range(TG):
                    with sp.Fori(0, C_STEPS) as e:
                        load(block_c(h, tg, e), wo[e])

        @block.gpsimd
        def _(pool):
            gp = nc.gpsimd
            gp.dma_start(cst[:, :], consts).then_inc(const_in, 16)
            gp.dma_start(ident[:, :], ident_d).then_inc(const_in, 16)
            gp.dma_start(rotm[:, :, :], rot_meta).then_inc(const_in, 16)
            gp.dma_start(wsum[0:META, 0:D], meta).then_inc(meta_in, 16)
            gp.dma_start(gainn[:, :], gain_n).then_inc(gn_in, 16)
            for t in range(4):
                gp.dma_start(xr[:, t, :], x[0, t]).then_inc(x_in[t], 16)
            gp.memset(kh[:, :, :].bitcast(F32), 0.0).then_inc(zero_r, 1)
            gp.memset(kl[:, :, :].bitcast(F32), 0.0).then_inc(s_done, CREDIT)
            gp.memset(vh[:, :, :].bitcast(F32), 0.0).then_inc(o_gate, CREDIT)
            gp.memset(vl[:, :, :].bitcast(F32), 0.0).then_inc(o_done, CREDIT)

            for h in range(HALVES):
                for t in range(4, NTT):
                    pool.wait_ge(z_t, NTT * h + t - 4 + MZ + 1)
                    gp.dma_start(xr[:, t - 4, :], x[h, t]).then_inc(x_in[t - 4], 16)
                if h > 0:
                    pool.wait_ge(c_done, 2 * NTT * h)
                gp.dma_start(cos_t[:, :], rot[h, 0]).then_inc(rot_tab, 16)
                gp.dma_start(sin_t[:, :], rot[h, 1]).then_inc(rot_tab, 16)
                pool.wait_ge(rot_tab, 32 * (h + 1))
                if h == 0:
                    pool.wait_ge(const_in, 48)

                def rotate(r, dst):
                    settle(pool)
                    pool.wait_ge(rot_sw, r + 1)
                    gp.tensor_tensor(rotsrc[:, :], rotsrc[:, :], cos_t[:, :], ALU.mult).then_inc(rot_mul, 1)
                    gp.tensor_tensor(swapped[:, :], swapped[:, :], sin_t[:, :], ALU.mult).then_inc(rot_mul, 1)
                    settle(pool)
                    pool.wait_ge(rot_mul, 2 * r + 2)
                    gp.tensor_tensor(dst, rotsrc[:, :].rearrange("p (c t) -> p c t", t=CH),
                                     swapped[:, :].rearrange("p (c t) -> p c t", t=CH), ALU.add).then_inc(rot_done, 1)

                if h > 0:
                    pool.wait_ge(gs_lo, C_BLOCKS * h)
                rotate((1 + HT) * h, qk[:, :, 0, :])
                if h == 0:
                    pool.wait_ge(km_sw, 1)
                    gp.tensor_tensor(km[:, :], km[:, :], rotm[:, 0, :], ALU.mult).then_inc(km_chain, 1)
                    gp.tensor_tensor(kms[:, :], kms[:, :], rotm[:, 1, :], ALU.mult).then_inc(km_chain, 1)
                    pool.wait_ge(km_chain, 2)
                    gp.tensor_tensor(km[:, :], km[:, :], kms[:, :], ALU.add).then_inc(km_chain, 1)
                    pool.wait_ge(km_chain, 3)
                    pool.wait_ge(zero_r, 1)
                    pool.wait_ge(s_done, 1)
                    for kv in range(2):
                        gp.tensor_tensor(kmm[:, kv, :], km[:, :], cst[:, kv:kv + 1].to_broadcast([P, META]), ALU.mult).then_inc(km_chain, 1)
                    pool.wait_ge(km_chain, 5)
                    gp.tensor_copy(kh[:, 0, META0:KPITCH].rearrange("p (k t) -> p k t", t=META), kmm[:, :, :]).then_inc(km_chain, 1)
                    pool.wait_ge(km_chain, 6)
                    gp.tensor_tensor(kl[:, 0, META0:KPITCH].rearrange("p (k t) -> p k t", t=META), kmm[:, :, :],
                                     kh[:, 0, META0:KPITCH].bitcast(F32).rearrange("p (k t) -> p k t", t=META), ALU.subtract).then_inc(km_done, 1)
                    pool.wait_ge(m_ev, 2)
                    for kv in range(2):
                        last = gp.tensor_tensor(vmm[:, META * kv:META * kv + META], vm[:, :], cst[:, kv:kv + 1].to_broadcast([P, META]), ALU.mult)
                    last.then_inc(vmm_r, 1)
                with pool.Fori(0, HT) as j:
                    rotate((1 + HT) * h + 1 + j, qk[:, :, 1 + j, :])
                pool.wait_ge(rot_done, (1 + HT) * (h + 1))
                gp.memset(ubuf[:, 0:PRE - META], 0.0).then_inc(u_halo, 1)

                with pool.Fori(0, NCH // 2) as pair:
                    for slot in range(2):
                        n = NCH * h + 2 * pair + slot
                        c = 2 * pair + slot
                        keys = slice(CH * slot, CH * slot + CH)
                        settle(pool)
                        pool.wait_ge(s_done, n + CREDIT)
                        gp.tensor_tensor(kmask[:, :, :], qk[:, c, 0:1, :].to_broadcast([P, 2, CH]),
                                         cst[:, 0:2].unsqueeze(2).to_broadcast([P, 2, CH]), ALU.mult).then_inc(ks_m, 1)
                        gp.tensor_copy(qh[:, :].rearrange("p (j t) -> p j t", t=CH), qk[:, c, 1:1 + HT, :]).then_inc(qs_hi, 1)
                        settle(pool)
                        pool.wait_ge(ks_m, n + 1)
                        gp.tensor_copy(kh[:, :, keys], kmask[:, :, :]).then_inc(ks_hi, 1)
                        settle(pool)
                        pool.wait_ge(qs_hi, n + 1)
                        gp.tensor_tensor(ql[:, :].rearrange("p (j t) -> p j t", t=CH), qk[:, c, 1:1 + HT, :],
                                         qh[:, :].bitcast(F32).rearrange("p (j t) -> p j t", t=CH), ALU.subtract).then_inc(qs_lo, 1)
                        settle(pool)
                        pool.wait_ge(ks_hi, n + 1)
                        gp.tensor_tensor(kl[:, :, keys], kmask[:, :, :], kh[:, :, keys].bitcast(F32), ALU.subtract).then_inc(qs_ready, 1)

                pool.wait_ge(pb_done[1], USES * (h + 1) - 2)
                gp.dma_start(hbuf[:, :, :], x[h].rearrange("t p d -> p t d")).then_inc(res_in, 16)
                pool.wait_ge(u_lo, PT * (h + 1))
                gp.dma_start(gainf[:, :], gain_f).then_inc(gf_in, 16)
                if h + 1 < HALVES:
                    pool.wait_ge(pb_done[1], USES * (h + 1))
                    gp.dma_start(gainn[:, :], gain_n).then_inc(gn_in, 16)
                    pool.wait_ge(o_done, NCH * (h + 1) + CREDIT)
                    for t in range(4):
                        gp.dma_start(xr[:, t, :], x[h + 1, t]).then_inc(x_in[t], 16)
                with pool.Fori(0, NTT) as t:
                    pool.wait_ge(f_out, NTT * h + t + 1)
                    gp.dma_start(out[h, t], hbuf[:, t, :]).then_inc(out_done, 16)
            pool.wait_ge(out_done, 16 * NTT * HALVES)

        @block.scalar
        def _(act):
            sc = nc.scalar

            def split_hi(h, pos, slot, size=1024):
                if isinstance(pos, tuple):
                    b = block_c(h, *pos)
                    slot_free_c(act, h, *pos)
                else:
                    b = BLOCKS * h + pos
                    slot_free(act, h, pos)
                act.wait_ge(w_in, 16 * (b + 1))
                sc.activation(wh[:, slot, 0:size], wraw[:, 0:size], ACT.Copy).then_inc(w_hi, 1)

            def square(src, junk, acc):
                return sc.activation(junk, src, ACT.Square, scale=1.0 / 32.0, accum_out=acc)

            split_hi(0, 0, 0)
            act.wait_ge(meta_in, 16)
            act.wait_ge(eps_r, 1)
            square(wsum[0:META, 0:D], ps[0:META, 4:6, :].rearrange("p b n -> p (b n)"), ssq[0:META, 0:1]).then_inc(z_ssq, 1)
            act.wait_ge(z_ssq, 1)
            sc.activation(std[0:META, 0:1], ssq[0:META, 0:1], ACT.Sqrt, bias=epst[0:META]).then_inc(z_std, 1)
            act.wait_ge(z_t, MZ)
            sc.activation(zmh[:, :, :], ps[:, PB[0], 0:KT * META].rearrange("p (k t) -> p k t", t=META), ACT.Copy).then_inc(z_hi, 1)

            for h in range(HALVES):
                def z_head(it, i):
                    T = NTT * h + 4 * it + i + MZ
                    act.wait_ge(x_in[i], 16 * (2 * h + it + 1))
                    square(xr[:, i, :], ps[:, 4:6, :].rearrange("p b n -> p (b n)"), ssq[:, i:i + 1]).then_inc(z_ssq, 1)
                    act.wait_ge(z_ssq, T + 1)
                    sc.activation(std[:, i:i + 1], ssq[:, i:i + 1], ACT.Sqrt, bias=epst).then_inc(z_std, 1)

                def z_tail(it, i):
                    T = NTT * h + 4 * it + i + MZ
                    act.wait_ge(z_t, T + 1)
                    bank = 2 * (i % 2)
                    sc.activation(zh[:, 4 * it + i, :, :].rearrange("p k t -> p (k t)"),
                                  ps[:, bank:bank + 2, :].rearrange("p b n -> p (b n)"), ACT.Copy).then_inc(z_hi, 1)

                if h > 0:
                    act.wait_ge(out_done, 16 * NTT * h)
                with act.Fori(0, 2) as it:
                    z_head(it, 0)
                    z_head(it, 1)
                    z_tail(it, 0)
                    z_head(it, 2)
                    z_tail(it, 1)
                    z_head(it, 3)
                    z_tail(it, 2)
                    z_tail(it, 3)

                def to_rotary(h, a, r):
                    for tb in range(NTB):
                        act.wait_ge(pb_done[tb], use_a(h, a) + 1)
                        if tb == 0 and not (isinstance(r, int) and r == 0):
                            act.wait_ge(rot_done, r)
                        i = sc.activation(rotsrc[:, tb * TB:tb * TB + TB], ps[:, PB[tb], :], ACT.Copy)
                        i.then_inc(rot_in, 1)

                split_hi(h, 1, 1)
                to_rotary(h, 0, (1 + HT) * h)
                if h == 0:
                    act.wait_ge(m_done, 1)
                    sc.activation(km[:, :], ps[:, SPARE, 0:META], ACT.Copy).then_inc(m_ev, 1)
                split_hi(h, 2, 0)
                for tb in range(NTB):
                    act.wait_ge(pb_done[tb], use_a(h, 1) + 1)
                    sc.activation(wsum[:, tb * TB:tb * TB + TB], ps[:, PB[tb], :], ACT.Copy).then_inc(v_in, 1)
                if h == 0:
                    act.wait_ge(m_done, 2)
                    sc.activation(vm[:, :], ps[:, SPARE, 0:META], ACT.Copy).then_inc(m_ev, 1)
                act.wait_ge(v_t, h + 1)
                sc.activation(vtok[:, :, :].rearrange("p m f -> p (m f)"), ps[:, 0:2, :].rearrange("p b n -> p (b n)"), ACT.Copy).then_inc(v_tok, 1)
                if h == 0:
                    act.wait_ge(vm_t, 1)
                    sc.activation(vmeta[0:32, :], ps[0:32, SPARE, 0:P], ACT.Copy)
                    sc.activation(vmeta[32:64, :], ps[0:32, SPARE, 0:P], ACT.Copy).then_inc(vm_hi, 1)

                def tanh(use, tb):
                    act.wait_ge(pb_done[tb], use + 1)
                    sc.activation(wsum[:, tb * TB:tb * TB + TB], ps[:, PB[tb], :], ACT.Tanh, scale=0.5).then_inc(tanh_r, 1)

                with act.Fori(0, HT) as j:
                    split_hi(h, 3 + 2 * j, 1)
                    to_rotary(h, 2 + 2 * j, (1 + HT) * h + 1 + j)
                    split_hi(h, 4 + 2 * j, 0)
                    for tb in range(NTB):
                        tanh(use_a(h, 3 + 2 * j), tb)

                with act.Fori(0, NG) as g:
                    for sub in range(4):
                        n = NCH * h + 4 * g + sub
                        split_hi(h, A_TILES + GROUP_BLOCKS * g + sub + 1, (sub + 1) % 2, size_b(sub + 1))
                        act.wait_ge(s_negm, n + 1)
                        for u in range(4):
                            for kv in range(2):
                                sc.activation(probs[:, u, kv * KEYS:kv * KEYS + KEYS], ps[:, u, kv * KEYS:kv * KEYS + KEYS], ACT.Exp,
                                              bias=negm[:, 2 * u + kv:2 * u + kv + 1], scale=SCALE,
                                              accum_out=den[:, 2 * u + kv:2 * u + kv + 1])
                        act.wait_ge(s_sarg, n + 1)
                        sc.activation(esink, sarg, ACT.Exp).then_inc(s_exp, 1)
                        if sub in (1, 2):
                            ut = PT * h + 2 * g + sub - 1
                            act.wait_ge(u_pool, ut + 1)
                            sc.activation(plh[:, sub - 1, :], wsum[:, META:META + TOK], ACT.Copy).then_inc(u_hi, 1)

                        def copy_out(tb):
                            if sub < 2:
                                act.wait_ge(pb_done[tb], use_b(h, g, sub) + 1)
                                if tb == 0:
                                    act.wait_ge(u_halo, (1 + PT) * h + 1 + 2 * g + sub + h)
                                sc.activation(ubuf[:, PRE + tb * TB:PRE + tb * TB + TB], ps[:, PB[tb], :], ACT.Copy).then_inc(u_in, 1)
                            else:
                                if sub == 2 and tb == 0:
                                    act.wait_ge(u_lo, PT * h + 2 * g + 2)
                                tanh(use_b(h, g, sub), tb)

                        copy_out(0)
                        if h == 0 and sub < 2:
                            act.wait_ge(m_done, 2 + 2 * g + sub + 1)
                            sc.activation(ubuf[:, PRE - META:PRE], ps[:, SPARE, 0:META], ACT.Copy).then_inc(m_ev, 1)
                        slot = sub % 2
                        lo_p, hi_p = slot * CH, slot * CH + CH
                        act.wait_ge(o_done, n + CREDIT)
                        sc.activation(vh[lo_p:hi_p, 0:4:3, :], vtok[lo_p:hi_p, 2 * g + sub // 2, :].rearrange("p (k d) -> p k d", k=2),
                                      ACT.Copy).then_inc(vw_hi, 1)
                        act.wait_ge(t_done, n + 1)
                        for kv in range(2):
                            sc.activation(pth[:, kv, :], ps[:, kv, :], ACT.Copy).then_inc(pt_hi, 1)
                        sc.activation(ptm[0:32, :], ps[0:32, 2, :], ACT.Copy).then_inc(pt_hi, 1)
                        sc.activation(ptm[64:96, :], ps[0:32, 2, :], ACT.Copy).then_inc(pt_hi, 1)
                        copy_out(1)
                    split_hi(h, A_TILES + GROUP_BLOCKS * g + 5, 1, SMALL)
                    split_hi(h, A_TILES + GROUP_BLOCKS * g + 6, 0)

                def gated_hi(tg, e, slot):
                    slot_free_c(act, h, tg, e)
                    sc.activation(gsh[:, slot, :], gates[:, e, tg * TB:tg * TB + TB], ACT.Copy).then_inc(gs_hi, 1)

                def final_stats(t):
                    k = NTT * h + t
                    act.wait_ge(h_add, 2 * (k + 1))
                    square(hbuf[:, t, :], wsum[:, 0:D], ssq[:, t % 4:t % 4 + 1]).then_inc(f_ssq, 1)
                    act.wait_ge(f_ssq, k + 1)
                    sc.activation(std[:, t % 4:t % 4 + 1], ssq[:, t % 4:t % 4 + 1], ACT.Sqrt, bias=epst).then_inc(f_std, 1)

                act.wait_ge(o_gate, NCH * (h + 1) + CREDIT)
                act.wait_ge(pb_free[0], FREES * (h + 1) + CREDIT)
                act.wait_ge(pb_free[1], FREES * (h + 1) + CREDIT)
                gated_hi(0, 0, 0)
                for tg in range(TG):
                    def step(e, slot):
                        split_hi(h, (tg, e + 1), 1 - slot)
                        gated_hi(tg, e + 1, 1 - slot)
                    step(0, 0)
                    if tg > 0:
                        for t in range(TPG):
                            final_stats((tg - 1) * TPG + t)
                    step(1, 1)
                    with act.Fori(1, C_STEPS // 2 - 1) as i:
                        step(2 * i, 0)
                        step(2 * i + 1, 1)
                    step(C_STEPS - 2, 0)
                    if block_c(h, tg, C_STEPS - 1) < LAST_BLOCK:
                        if tg + 1 < TG:
                            split_hi(h, (tg + 1, 0), 0)
                        else:
                            split_hi(h + 1, 0, 0)
                    if tg + 1 < TG:
                        gated_hi(tg + 1, 0, 0)
                for t in range(TPG):
                    final_stats((TG - 1) * TPG + t)

        @block.vector
        def _(dve):
            ve = nc.vector

            def split_lo(b, slot, size=1024):
                dve.wait_ge(w_hi, b + 1)
                ve.tensor_tensor(wl[:, slot, 0:size], wraw[:, 0:size], wh[:, slot, 0:size].bitcast(F32), ALU.subtract).then_inc(w_lo, 1)

            def hold():
                ve.memset(small[:, 13:14], 0.0)

            for tb in range(NTB):
                ve.memset(small[:, 14 + tb:15 + tb], 0.0).then_inc(pb_free[tb], CREDIT)
            ve.memset(epst, EPS).then_inc(eps_r, 1)
            dve.wait_ge(const_in, 48)
            ve.tensor_scalar(pgate, pscale, 0.5, None, ALU.mult).then_inc(psc_r, 1)
            ve.tensor_scalar(nsinks, sinks, -1.0, None, ALU.mult).then_inc(psc_r, 1)
            dve.wait_ge(psc_r, 2)
            split_lo(0, 0)
            dve.wait_ge(z_std, 1)
            dve.wait_ge(gn_in, 16)
            ve.reciprocal(rstd[0:META, 0:1], std[0:META, 0:1]).then_inc(z_rstd, 1)
            dve.wait_ge(z_rstd, 1)
            ve.scalar_tensor_tensor(wsum[0:META, 0:D], wsum[0:META, 0:D], rstd[0:META, 0:1], gainn[0:META, :], ALU.mult, ALU.mult).then_inc(z_norm, 1)
            dve.wait_ge(z_hi, 1)
            ve.tensor_tensor(zml[:, :, :], ps[:, PB[0], 0:KT * META].rearrange("p (k t) -> p k t", t=META), zmh[:, :, :].bitcast(F32), ALU.subtract).then_inc(z_lo, 1)

            for h in range(HALVES):
                if h > 0:
                    dve.wait_ge(gn_in, 16 * (h + 1))

                def z_head(it, i):
                    T = NTT * h + 4 * it + i + MZ
                    dve.wait_ge(z_std, T + 1)
                    ve.reciprocal(rstd[:, i:i + 1], std[:, i:i + 1]).then_inc(z_rstd, 1)
                    dve.wait_ge(z_rstd, T + 1)
                    ve.scalar_tensor_tensor(xr[:, i, :], xr[:, i, :], rstd[:, i:i + 1], gainn[:, :], ALU.mult, ALU.mult).then_inc(z_norm, 1)

                def z_tail(it, i):
                    T = NTT * h + 4 * it + i + MZ
                    dve.wait_ge(z_hi, T + 1)
                    bank = 2 * (i % 2)
                    ve.tensor_tensor(zl[:, 4 * it + i, :, :].rearrange("p k t -> p (k t)"),
                                     ps[:, bank:bank + 2, :].rearrange("p b n -> p (b n)"),
                                     zh[:, 4 * it + i, :, :].rearrange("p k t -> p (k t)").bitcast(F32), ALU.subtract).then_inc(z_lo, 1)

                with dve.Fori(0, 2) as it:
                    z_head(it, 0)
                    z_head(it, 1)
                    z_tail(it, 0)
                    z_head(it, 2)
                    z_tail(it, 1)
                    z_head(it, 3)
                    z_tail(it, 2)
                    z_tail(it, 3)

                SWAP = [(i + 8) % 16 if i < 16 else i for i in range(32)]

                def swap(r):
                    dve.wait_ge(rot_in, 2 * r + 2)
                    hold()
                    ve.stream_shuffle(swapped[:, :], rotsrc[:, :], SWAP).then_inc(rot_sw, 1)

                def silu(dst, use, count, tb):
                    dve.wait_ge(tanh_r, count)
                    ve.scalar_tensor_tensor(dst, wsum[:, tb * TB:tb * TB + TB], 1.0, ps[:, PB[tb], :], ALU.add, ALU.mult).then_inc(pb_free[tb], 1)

                split_lo(block_a(h, 1), 1)
                swap((1 + HT) * h)
                if h == 0:
                    dve.wait_ge(m_ev, 1)
                    ve.stream_shuffle(kms[:, :], km[:, :], SWAP).then_inc(km_sw, 1)
                split_lo(block_a(h, 2), 0)
                if h == 0:
                    dve.wait_ge(vm_hi, 1)
                    ve.tensor_tensor(vmeta[64:96, :], ps[0:32, SPARE, 0:P], vmeta[0:32, :].bitcast(F32), ALU.subtract).then_inc(vm_done, 1)
                with dve.Fori(0, HT) as j:
                    split_lo(block_a(h, 3 + 2 * j), 1)
                    swap((1 + HT) * h + 1 + j)
                    split_lo(block_a(h, 4 + 2 * j), 0)
                    for tb in range(NTB):
                        silu(gates[:, j, tb * TB:tb * TB + TB], use_a(h, 3 + 2 * j), (2 * HT + 2 * PT) * h + 2 * j + tb + 1, tb)

                with dve.Fori(0, NG) as g:
                    for sub in range(4):
                        n = NCH * h + 4 * g + sub
                        scores = ps[:, 0:4, 0:2 * KEYS].rearrange("p u (k s) -> p u k s", k=2)
                        dve.wait_ge(s_done, n + 1 + CREDIT)
                        if h == 0 and sub == 0:
                            for kv in range(2):
                                empty = ps[:, 0:4, kv * KPITCH + CH:kv * KPITCH + 2 * CH]
                                i = ve.tensor_scalar(empty, empty, cst[:, bass.ds(6 + g, 1)], None, ALU.add)
                                i.then_inc(s_mask, 1)
                            dve.wait_ge(s_mask, 2 * (g + 1))
                        ve.tensor_reduce(mx, scores, AXX, ALU.max).then_inc(s_max, 1)
                        dve.wait_ge(s_max, n + 1)
                        ve.scalar_tensor_tensor(negm, mx, -SCALE, nsinks, ALU.mult, ALU.min).then_inc(s_negm, 1)
                        dve.wait_ge(s_negm, n + 1)
                        ve.tensor_tensor(sarg, negm, sinks, ALU.add).then_inc(s_sarg, 1)
                        if sub in (1, 2):
                            ut = PT * h + 2 * g + sub - 1
                            dve.wait_ge(u_in, 2 * ut + 2)
                            if h == 0:
                                dve.wait_ge(m_ev, 2 + ut + 1)
                            hold()
                            ve.tensor_tensor_scan(wsum[:, :], ubuf[:, META:PRE + TOK], ubuf[:, bass.ds(META - (2 << g), META + TOK)], 0.0,
                                                  ALU.add, ALU.subtract).then_inc(u_sum, 1)
                            dve.wait_ge(u_sum, ut + 1)
                            ve.scalar_tensor_tensor(wsum[:, META:META + TOK], wsum[:, META:META + TOK], cst[:, bass.ds(2 + g, 1)],
                                                    ubuf[:, PRE:PRE + TOK], ALU.mult, ALU.subtract).then_inc(u_pool, 1)
                            if h == 0:
                                ve.tensor_copy(halo[:, 2 * g + sub - 1, :], ubuf[:, TOK + PRE - META:TOK + PRE]).then_inc(u_halo, 1)
                        if h > 0 and sub < 2:
                            dve.wait_ge(u_halo, 1 + PT + 1 + 2 * g + sub)
                            ve.tensor_copy(ubuf[:, PRE - META:PRE], halo[:, 2 * g + sub, :]).then_inc(u_halo, 1)
                        split_lo(block_b(h, g, sub + 1), (sub + 1) % 2, size_b(sub + 1))
                        dve.wait_ge(s_exp, n + 1)
                        ve.tensor_tensor(dsum, den, esink, ALU.add).then_inc(d_sum, 1)
                        dve.wait_ge(d_sum, n + 1)
                        ve.reciprocal(rden, dsum).then_inc(d_rcp, 1)
                        dve.wait_ge(d_rcp, n + 1)
                        pr = probs[:, :, :].rearrange("p u (k s) -> p (u k) s", k=2)
                        ve.tensor_tensor(pr, pr, rden.unsqueeze(2).to_broadcast([P, 8, KEYS]), ALU.mult).then_inc(p_ready, 1)
                        if sub in (1, 2):
                            dve.wait_ge(u_hi, ut + 1)
                            ve.tensor_tensor(pll[:, sub - 1, :], wsum[:, META:META + TOK], plh[:, sub - 1, :].bitcast(F32), ALU.subtract).then_inc(u_lo, 1)

                        def gate_tile(tb):
                            if sub >= 2:
                                silu(gates[:, HT + 2 * g + sub - 2, tb * TB:tb * TB + TB], None,
                                     (2 * HT + 2 * PT) * h + 2 * HT + 2 * (2 * g + sub - 2) + tb + 1, tb)

                        gate_tile(0)
                        slot = sub % 2
                        lo_p, hi_p = slot * CH, slot * CH + CH
                        dve.wait_ge(vw_hi, n + 1)
                        ve.tensor_tensor(vl[lo_p:hi_p, 0:4:3, :], vtok[lo_p:hi_p, 2 * g + sub // 2, :].rearrange("p (k d) -> p k d", k=2),
                                         vh[lo_p:hi_p, 0:4:3, :].bitcast(F32), ALU.subtract).then_inc(vw_lo, 1)
                        for kv in range(2):
                            dve.wait_ge(pt_hi, 4 * n + kv + 1)
                            ve.tensor_tensor(ptl[:, kv, :], ps[:, kv, :], pth[:, kv, :].bitcast(F32), ALU.subtract)
                        dve.wait_ge(pt_hi, 4 * n + 4)
                        ve.tensor_tensor(ptm[32:64, :], ps[0:32, 2, :], ptm[0:32, :].bitcast(F32), ALU.subtract).then_inc(pt_lo, 1)
                        gate_tile(1)
                        dve.wait_ge(o_done, n + 1 + CREDIT)
                        gslice = gates[:, 0:HT, bass.ds((4 * g + sub) * CH, CH)]
                        ve.scalar_tensor_tensor(gslice, ps[:, OB, :].rearrange("p (j t) -> p j t", t=CH), 0.5, gslice, ALU.mult, ALU.mult).then_inc(o_gate, 1)
                    split_lo(block_b(h, g, 5), 1, SMALL)
                    for dt in range(2):
                        if dt == 1:
                            split_lo(block_b(h, g, 6), 0)
                        for tb in range(NTB):
                            dve.wait_ge(pb_done[tb], use_b(h, g, 4 + dt) + 1)
                            gt = gates[:, HT + 2 * g + dt, tb * TB:tb * TB + TB]
                            ve.scalar_tensor_tensor(gt, ps[:, PB[tb], :], stat[:, bass.ds(56 + 2 * g + dt, 1)], gt, ALU.mult, ALU.mult).then_inc(pb_free[tb], 1)

                def gated_lo(tg, e, slot):
                    b = C_BLOCKS * h + C_STEPS * tg + e
                    dve.wait_ge(gs_hi, b + 1)
                    ve.tensor_tensor(gsl[:, slot, :], gates[:, e, tg * TB:tg * TB + TB], gsh[:, slot, :].bitcast(F32), ALU.subtract).then_inc(gs_lo, 1)

                def add_rows(tg):
                    for t in range(TPG):
                        for dh in range(2):
                            k = NTT * h + tg * TPG + t
                            dve.wait_ge(c_done, 2 * k + dh + 1)
                            hs = hbuf[:, tg * TPG + t, dh * TB:dh * TB + TB]
                            ve.tensor_tensor(hs, ps[:, 2 * t + dh, :], hs, ALU.add).then_inc(h_add, 1)

                def final_rows(t):
                    k = NTT * h + t
                    dve.wait_ge(f_std, k + 1)
                    ve.reciprocal(rstd[:, t % 4:t % 4 + 1], std[:, t % 4:t % 4 + 1]).then_inc(f_rstd, 1)
                    dve.wait_ge(f_rstd, k + 1)
                    ve.scalar_tensor_tensor(hbuf[:, t, :], hbuf[:, t, :], rstd[:, t % 4:t % 4 + 1], gainf[:, :], ALU.mult, ALU.mult).then_inc(f_out, 1)

                gated_lo(0, 0, 0)
                for tg in range(TG):
                    def step(e, slot):
                        split_lo(block_c(h, tg, e) + 1, 1 - slot)
                        gated_lo(tg, e + 1, 1 - slot)
                    step(0, 0)
                    if tg == 0:
                        dve.wait_ge(res_in, 16 * (h + 1))
                        dve.wait_ge(gf_in, 16 * (h + 1))
                    else:
                        for t in range(TPG):
                            final_rows((tg - 1) * TPG + t)
                    step(1, 1)
                    with dve.Fori(1, C_STEPS // 2 - 1) as i:
                        step(2 * i, 0)
                        step(2 * i + 1, 1)
                    step(C_STEPS - 2, 0)
                    if block_c(h, tg, C_STEPS - 1) < LAST_BLOCK:
                        split_lo(block_c(h, tg, C_STEPS - 1) + 1, 0)
                    if tg + 1 < TG:
                        gated_lo(tg + 1, 0, 0)
                    add_rows(tg)
                for t in range(TPG):
                    final_rows((TG - 1) * TPG + t)

        @block.tensor
        def _(pe):
            te = nc.tensor

            def rhs_z(z, tb, k):
                return z[:, tb * (TB // P):(tb + 1) * (TB // P), k, :]

            def project(slot, tb, k0, k1):
                for k in range(k0, k1):
                    w_h, w_l = wh[:, slot, k * P:k * P + P], wl[:, slot, k * P:k * P + P]
                    te.matmul(ps[:, PB[tb], :], w_h, rhs_z(zh, tb, k), start=k == 0, stop=False)
                    te.matmul(ps[:, PB[tb], :], w_h, rhs_z(zl, tb, k), start=False, stop=False)
                    last = te.matmul(ps[:, PB[tb], :], w_l, rhs_z(zh, tb, k), start=False, stop=k == KT - 1)
                if k1 == KT:
                    last.then_inc(pb_done[tb], 1)
                return last

            def project_meta(slot):
                for k in range(KT):
                    w_h, w_l = wh[:, slot, k * P:k * P + P], wl[:, slot, k * P:k * P + P]
                    te.matmul(ps[:, SPARE, 0:META], w_h, zmh[:, k, :], start=k == 0, stop=False)
                    te.matmul(ps[:, SPARE, 0:META], w_h, zml[:, k, :], start=False, stop=False)
                    last = te.matmul(ps[:, SPARE, 0:META], w_l, zmh[:, k, :], start=False, stop=k == KT - 1)
                last.then_inc(m_done, 1)
                return last

            pe.wait_ge(const_in, 48)
            pe.wait_ge(z_norm, 1)
            for k in range(KT):
                last = te.transpose(ps[:, PB[0], k * META:k * META + META], wsum[0:META, k * P:k * P + P], ident[0:META, 0:META])
            last.then_inc(z_t, 1)

            for h in range(HALVES):
                if h > 0:
                    pe.wait_ge(h_add, 2 * NTT * h)
                with pe.Fori(0, 2) as it:
                    for i in range(4):
                        T = NTT * h + 4 * it + i + MZ
                        pe.wait_ge(z_norm, T + 1)
                        pe.wait_ge(z_lo, T - (i > 0))
                        for k in range(KT):
                            last = te.transpose(ps[:, 2 * (i % 2) + k // 4, (k % 4) * P:(k % 4) * P + P], xr[:, i, k * P:k * P + P], ident[:, :])
                        last.then_inc(z_t, 1)

                def tile_a(a, slot, bank_free=None, meta_too=False):
                    pe.wait_ge(w_lo, block_a(h, a) + 1)
                    for tb in range(NTB):
                        if bank_free:
                            bank_free(tb)
                        project(slot, tb, 0, KT)
                        if tb == 0 and meta_too:
                            if a == 1:
                                pe.wait_ge(m_ev, 1)
                            project_meta(slot)

                pe.wait_ge(z_lo, NTT * (h + 1) + MZ)
                tile_a(0, 0, None, h == 0)
                tile_a(1, 1, lambda tb: pe.wait_ge(rot_in, 2 * (1 + HT) * h + tb + 1), h == 0)
                pe.wait_ge(v_in, 2 * (h + 1))
                for m in range(NTT):
                    last = te.transpose(ps[:, m // 4, (m % 4) * P:(m % 4) * P + P], wsum[:, m * P:m * P + P], ident[:, :])
                last.then_inc(v_t, 1)
                if h == 0:
                    pe.wait_ge(vmm_r, 1)
                    te.transpose(ps[0:32, SPARE, 0:P], vmm[:, :], ident[:, :]).then_inc(vm_t, 1)
                with pe.Fori(0, HT) as j:
                    tile_a(2 + 2 * j, 0, lambda tb: pe.wait_ge(pb_free[tb], FREES * h + j + CREDIT))
                    tile_a(3 + 2 * j, 1, lambda tb: pe.wait_ge(rot_in, 2 * ((1 + HT) * h + 1 + j) + tb + 1))

                if h == 0:
                    pe.wait_ge(km_done, 1)
                    pe.wait_ge(vm_done, 1)
                with pe.Fori(0, NG) as g:
                    for sub in range(4):
                        n = NCH * h + 4 * g + sub
                        slot = sub % 2
                        pe.wait_ge(qs_ready, n + 1)
                        for u in range(4):
                            q_h, q_l = qh[:, u * P:u * P + P], ql[:, u * P:u * P + P]
                            so = ps[:, u, 0:2 * KEYS]
                            k_h, k_l = (w[:, :, :].rearrange("p k s -> p (k s)")[:, 0:2 * KEYS] for w in (kh, kl))
                            te.matmul(so, q_h, k_h, start=True, stop=False)
                            te.matmul(so, q_h, k_l, start=False, stop=False)
                            last = te.matmul(so, q_l, k_h, start=False, stop=True)
                        last.then_inc(s_done, 1)
                        pe.wait_ge(w_lo, block_b(h, g, sub) + 1)
                        ut = PT * h + 2 * g + sub

                        def bank_free(tb):
                            if sub in (1, 2):
                                pe.wait_ge(u_in, 2 * (ut - 1) + tb + 1)
                            else:
                                pe.wait_ge(pb_free[tb], FREES * h + HT + 4 * g + sub // 3 + CREDIT)

                        bank_free(0)
                        project(slot, 0, 0, KT)
                        if h == 0 and sub < 2:
                            pe.wait_ge(m_ev, 2 + 2 * g + sub)
                            project_meta(slot)
                        bank_free(1)
                        project(slot, 1, 0, 3)
                        pe.wait_ge(p_ready, n + 1)
                        for kv in range(2):
                            for u in range(4):
                                te.transpose(ps[:, kv, u * P:u * P + P], probs[:, u, kv * KPITCH:kv * KPITCH + 2 * CH], ident[:, :])
                        for u in range(4):
                            last = te.transpose(ps[0:32, 2, u * P:u * P + P], probs[:, u, META0:KPITCH], ident[:, :])
                        last.then_inc(t_done, 1)
                        project(slot, 1, 3, KT)
                        pe.wait_ge(pt_lo, n + 1)
                        pe.wait_ge(vw_lo, n + 1)
                        pe.wait_ge(o_gate, n + CREDIT)
                        ob = ps[:, OB, :]
                        for kv in range(2):
                            v_h = vh[:, 2 * kv:2 * kv + 2, :].rearrange("p a d -> p (a d)")
                            v_l = vl[:, 2 * kv:2 * kv + 2, :].rearrange("p a d -> p (a d)")
                            te.matmul(ob, v_h, pth[:, kv, :], start=kv == 0, stop=False)
                            te.matmul(ob, v_h, ptl[:, kv, :], start=False, stop=False)
                            te.matmul(ob, v_l, pth[:, kv, :], start=False, stop=False)
                        te.matmul(ob, vmeta[0:96, :], ptm[0:96, :], start=False, stop=True).then_inc(o_done, 1)
                    for dt in range(2):
                        pe.wait_ge(w_lo, block_b(h, g, 4 + dt) + 1)
                        pe.wait_ge(u_lo, PT * h + 2 * g + 2)
                        for tb in range(NTB):
                            pe.wait_ge(pb_free[tb], FREES * h + HT + 4 * g + 2 + dt + CREDIT)
                            mo = ps[:, PB[tb], :]
                            for ct in range(2):
                                m_h, m_l = wh[:, dt, ct * P:ct * P + P], wl[:, dt, ct * P:ct * P + P]
                                te.matmul(mo, m_h, plh[:, ct, tb * TB:tb * TB + TB], start=ct == 0, stop=False)
                                te.matmul(mo, m_h, pll[:, ct, tb * TB:tb * TB + TB], start=False, stop=False)
                                last = te.matmul(mo, m_l, plh[:, ct, tb * TB:tb * TB + TB], start=False, stop=ct == 1)
                            last.then_inc(pb_done[tb], 1)

                for tg in range(TG):
                    def step(e, slot, first=False, final=False):
                        pe.wait_ge(w_lo, block_c(h, tg, e) + 1)
                        pe.wait_ge(gs_lo, C_BLOCKS * h + C_STEPS * tg + e + 1)
                        for t in range(TPG):
                            g_h, g_l = gsh[:, slot, t * P:t * P + P], gsl[:, slot, t * P:t * P + P]
                            for dh in range(2):
                                if first and tg > 0:
                                    pe.wait_ge(h_add, 2 * (NTT * h + (tg - 1) * TPG + t) + dh + 1)
                                w_h, w_l = wh[:, slot, dh * TB:dh * TB + TB], wl[:, slot, dh * TB:dh * TB + TB]
                                co = ps[:, 2 * t + dh, :]
                                te.matmul(co, g_h, w_h, start=first, stop=False)
                                te.matmul(co, g_h, w_l, start=False, stop=False)
                                last = te.matmul(co, g_l, w_h, start=False, stop=final)
                                if final:
                                    last.then_inc(c_done, 1)
                        if not final:
                            last.then_inc(c_used, 1)

                    if tg == 0:
                        for tb in range(NTB):
                            pe.wait_ge(pb_free[tb], FREES * (h + 1) + CREDIT)
                        pe.wait_ge(o_gate, NCH * (h + 1) + CREDIT)
                    step(0, 0, first=True)
                    step(1, 1)
                    with pe.Fori(1, C_STEPS // 2 - 1) as i:
                        step(2 * i, 0)
                        step(2 * i + 1, 1)
                    step(C_STEPS - 2, 0)
                    step(C_STEPS - 1, 1, final=True)


_INS = ["x", "meta", "wa", "wb", "wp", "wo", "gain_n", "gain_f", "consts", "ident", "rot", "rot_meta"]


def rotary_tables():
    half = HD // 4 // 2
    inv = (np.float32(500000.0) ** (-np.arange(half, dtype=np.float32) * np.float32(2.0 / (HD // 4)))).astype(np.float32)
    ang = np.arange(META + SEQ, dtype=np.float32)[None, :] * inv[:, None]
    cos, sin = np.cos(ang).astype(np.float32), np.sin(ang).astype(np.float32)
    c = np.ones((HD, META + SEQ), np.float32)
    s = np.zeros((HD, META + SEQ), np.float32)
    c[0:half], c[half:2 * half] = cos, cos
    s[0:half], s[half:2 * half] = -sin, sin
    return np.concatenate([c, c]), np.concatenate([s, s])


def kernel(x, meta_tokens, norm_gain, w_in, attn_sinks, w_pool, pool_scale, w_out, final_norm_gain):
    import concourse.bacc as bacc
    from concourse.bass_utils import run_bass_kernel_spmd

    w = np.asarray(w_in)[0]
    pairs = [np.r_[j * HD:(j + 1) * HD, (HT + j) * HD:(HT + j + 1) * HD] for j in range(HT)]
    q0, k0, v0, g0 = 0, HT * P, HT * P + P, HT * P + 2 * P
    u0 = g0 + HT * P
    p0 = u0 + PT * P

    def tiles(cols):
        t = w[:, np.stack(cols)]
        return np.ascontiguousarray(t.reshape(KT, P, len(cols), P).transpose(2, 1, 0, 3).reshape(len(cols), P, KT * P))

    cols = [np.arange(k0, k0 + P), np.arange(v0, v0 + P)]
    for j in range(HT):
        cols += [q0 + pairs[j], g0 + pairs[j]]
    wa = tiles(cols)
    cols = []
    for g in range(NG):
        for first in (u0, p0):
            cols += [np.arange(first + (2 * g + i) * P, first + (2 * g + i + 1) * P) for i in range(2)]
    wb = tiles(cols).reshape(NG, 4, P, KT * P)
    wp = np.ascontiguousarray(np.asarray(w_pool)[0].reshape(NG, 2, P, 2, P).transpose(0, 3, 2, 1, 4).reshape(NG, 2, P, 2 * P))
    rows = np.concatenate(pairs + [HT * P + np.arange(PT * P)])
    wo = np.ascontiguousarray(np.asarray(w_out)[0][rows].reshape(C_STEPS, P, D))

    consts = np.zeros((P, 32), np.float32)
    consts[:HD, 0] = 1.0
    consts[HD:, 1] = 1.0
    consts[:, 2:6] = [0.5, 0.25, 0.125, 0.0625]
    consts[:, 6] = -1e30
    sinks = np.asarray(attn_sinks)[0]
    for u in range(4):
        for kv in range(2):
            for i in range(2):
                consts[i * CH:(i + 1) * CH, 10 + 2 * u + kv] = sinks[kv * 8 + 2 * u + i]
    consts[:, 18:26] = np.asarray(pool_scale)[0].reshape(PT, P).T
    cos, sin = rotary_tables()
    rot = np.stack([np.stack([t[:, META + h * TOK:META + (h + 1) * TOK] for t in (cos, sin)]) for h in range(HALVES)])
    rot_meta = np.stack([cos[:, :META], sin[:, :META]], axis=1)

    arrays = {
        "x": np.asarray(x)[0].reshape(HALVES, NTT, P, D),
        "meta": np.asarray(meta_tokens),
        "wa": wa, "wb": wb, "wp": wp, "wo": wo,
        "gain_n": np.broadcast_to(np.asarray(norm_gain)[0], (P, D)),
        "gain_f": np.broadcast_to(np.asarray(final_norm_gain), (P, D)),
        "consts": consts, "ident": np.eye(P, dtype=np.float32), "rot": rot, "rot_meta": rot_meta,
    }
    nc = bacc.Bacc("TRN2", target_bir_lowering=False, num_devices=1)
    ins, args = {}, []
    for name in _INS:
        a = np.ascontiguousarray(arrays[name])
        ins[f"in_{name}"] = a
        args.append(nc.dram_tensor(f"in_{name}", a.shape, mybir.dt.from_np(a.dtype), kind="ExternalInput").ap())
    out = nc.dram_tensor("out_y", (HALVES, NTT, P, D), F32, kind="ExternalOutput").ap()
    build(nc, *args, out)
    r = run_bass_kernel_spmd(nc, [ins], core_ids=[0])
    return r.results[0]["out_y"].reshape(1, SEQ, D)
```

```python
from contextlib import ExitStack

import numpy as np

import concourse.bass as bass
from concourse import mybir

F32 = mybir.dt.float32
F32R = mybir.dt.float32r
ACT = mybir.ActivationFunctionType
ALU = mybir.AluOpType
AXX = mybir.AxisListType.X

P = 128
D = 1024
KT = D // P
SEQ = 2048
META = 16
CH = 64
HD = 64
HALVES = 2
TOK = SEQ // HALVES
NTT = TOK // P
NCH = TOK // CH
TB = 512
NTB = TOK // TB
HT = 8
PT = 8
NG = 4
KEYS = META + 2 * CH
KPITCH = KEYS + META
META0 = 2 * CH
EPS = 1e-6
SCALE = HD ** -0.5
PRE = 32

A_TILES = 2 + 2 * HT
GROUP_BLOCKS = 6
B_BLOCKS = NG * GROUP_BLOCKS
C_STEPS = HT + PT
TG = 2
TPG = NTT // TG
C_BLOCKS = TG * C_STEPS
BLOCKS = A_TILES + B_BLOCKS + C_BLOCKS
USES = A_TILES + B_BLOCKS
FREES = HT + 4 * NG


def build(nc, x, meta, wa, wb, wp, wo, gain_n, gain_f, consts, ident_d, rot, rot_meta, out):
    ctx = ExitStack()
    with ctx:
        base = 16512
        arena = ctx.enter_context(nc.sbuf_tensor("arena", [P, (229344 - base - 64) // 4], F32))
        cursor = [base]

        def at(offset, name, shape, dt=F32):
            return nc.alloc_sbuf_tensor_at(name, shape, dt, offset=offset)

        def place(name, shape, dt=F32):
            size = 4 * int(np.prod(shape[1:]))
            offset = cursor[0]
            cursor[0] += (size + 31) // 32 * 32
            return at(offset, name, shape, dt), offset

        zh, zh_at = place("zh", [P, NTT, KT, P], F32R)
        zl, zl_at = place("zl", [P, NTT, KT, P], F32R)
        rows_in = [at(offset + 4 * TPG * D, name, [P, TPG, D]) for name, offset in (("rows0", zh_at), ("rows1", zl_at))]
        gates, g_at = place("gates", [P, HT, TOK])
        rows = [rows_in[0], at(g_at, "rows1_out", [P, TPG, D])]
        meta_rows = at(g_at, "meta_rows", [META, D])
        qk, qk_at = place("qk", [P, NCH, 1 + HT, CH])
        gates = at(g_at, "gates_all", [P, HT + PT, TOK])
        wraw, _ = place("wraw", [P, 2, 1024])
        wh, _ = place("wh", [P, 2, 1024], F32R)
        wl, _ = place("wl", [P, 2, 1024], F32R)
        plh, pool_at = place("plh", [P, 2, TOK], F32R)
        pll, _ = place("pll", [P, 2, TOK], F32R)
        cos_t = at(pool_at, "cos_t", [P, TOK])
        sin_t = at(pool_at + 4096, "sin_t", [P, TOK])
        gsh = at(pool_at, "gsh", [P, 2, TB], F32R)
        gsl = at(pool_at + 4096, "gsl", [P, 2, TB], F32R)
        gainn = at(pool_at + 8192, "gainn", [P, D])
        swapped = at(pool_at + 12288, "swapped", [P, TOK])
        r_at = cursor[0]
        pth, pth_at = place("pth", [P, 2, TB], F32R)
        ptl, _ = place("ptl", [P, 2, TB], F32R)
        probs = at(pth_at, "probs", [P, 4, 2 * KEYS])
        ptm, _ = place("ptm", [P, TB], F32R)
        qh, _ = place("qh", [P, HT * CH], F32R)
        ql, _ = place("ql", [P, HT * CH], F32R)
        kmask, _ = place("kmask", [P, 2, CH])
        km, _ = place("km", [P, META])
        kms, _ = place("kms", [P, META])
        kmm, _ = place("kmm", [P, 2, META])
        vm, _ = place("vm", [P, META])
        vmm, _ = place("vmm", [P, 2 * META])
        assert cursor[0] <= r_at + 4 * 4096
        xr = at(r_at, "xr", [P, 4, D])
        cursor[0] = r_at + 4 * 4096
        ubuf, u_at = place("ubuf", [P, PRE + TOK])
        rotsrc = at(u_at, "rotsrc", [P, TOK])
        wsum, _ = place("wsum", [P, META + TOK])
        vtok, vtok_at = place("vtok", [P, NTT, P])
        gainf = at(vtok_at, "gainf", [P, D])
        kh, _ = place("kh", [P, 2, KPITCH], F32R)
        kl, _ = place("kl", [P, 2, KPITCH], F32R)
        vh, _ = place("vh", [P, 4, HD], F32R)
        vl, _ = place("vl", [P, 4, HD], F32R)
        vmeta, _ = place("vmeta", [P, P], F32R)
        ident, _ = place("ident", [P, P])
        halo, _ = place("halo", [P, PT, META])
        zmh, _ = place("zmh", [P, KT, META], F32R)
        zml, _ = place("zml", [P, KT, META], F32R)
        cst, _ = place("cst", [P, 32])
        rotm, _ = place("rotm", [P, 2, META])
        stat, _ = place("stat", [P, 72])
        small, _ = place("small", [P, 16])
        assert cursor[0] <= 229344, cursor[0]
        kvmask, invw, negfirst = cst[:, 0:2], cst[:, 2:6], cst[:, 6:10]
        sinks, pscale = cst[:, 10:18], cst[:, 18:26]
        mx, negm, sarg, esink = (stat[:, 8 * i:8 * i + 8] for i in range(4))
        den, dsum, rden, pgate = (stat[:, 8 * i:8 * i + 8] for i in range(4, 8))
        f_ss, f_sd, f_rs = (stat[:, 8 * i:8 * i + 4] for i in range(3))
        ssq, std, rstd = small[:, 0:4], small[:, 4:8], small[:, 8:12]
        epst = small[:, 12:13]
        nsinks = stat[:, 64:72]

        ps = ctx.enter_context(nc.psum_tensor("ps", [P, 8, TB], F32))
        OB, SPARE, PB = 4, 5, (6, 7)

        def sem(name):
            return ctx.enter_context(nc.semaphore(name))

        const_in = sem("const_in")
        meta_in = sem("meta_in")
        gn_first, gn_in = sem("gn_first"), sem("gn_in")
        gf_in = sem("gf_in")
        rot_tab = sem("rot_tab")
        x_first = [sem(f"x_first{i}") for i in range(4)]
        x_in = [sem(f"x_in{i}") for i in range(4)]
        res_in = sem("res_in")
        w_in = [sem(f"w_in{i}") for i in range(2)]
        out_done = [sem(f"out_done{i}") for i in range(TG)]
        zm_step = sem("zm_step")
        z_ssq, z_std, z_rstd, z_norm, z_t, z_hi, z_lo = (sem("z_" + n) for n in ("ssq", "std", "rstd", "norm", "t", "hi", "lo"))
        w_hi, w_lo, c_used = sem("w_hi"), sem("w_lo"), sem("c_used")
        pb_done = [sem(f"pb_done{i}") for i in range(2)]
        pb_free = [sem(f"pb_free{i}") for i in range(2)]
        rot_in, rot_sw, rot_mul, rot_done = sem("rot_in"), sem("rot_sw"), sem("rot_mul"), sem("rot_done")
        v_in, v_t, v_tok = sem("v_in"), sem("v_t"), sem("v_tok")
        vmm_r, vm_t, vm_hi, vm_done = sem("vmm_r"), sem("vm_t"), sem("vm_hi"), sem("vm_done")
        m_done, m_ev = sem("m_done"), sem("m_ev")
        km_sw, km_chain, km_done = sem("km_sw"), sem("km_chain"), sem("km_done")
        tanh_r = sem("tanh_r")
        s_done, s_mask, s_max, s_negm, s_sarg, s_exp = (sem("s_" + n) for n in ("done", "mask", "max", "negm", "sarg", "exp"))
        d_sum, d_rcp, p_ready, t_done = sem("d_sum"), sem("d_rcp"), sem("p_ready"), sem("t_done")
        pt_hi, pt_lo = sem("pt_hi"), sem("pt_lo")
        o_done, o_gate = sem("o_done"), sem("o_gate")
        qs_hi, qs_lo, ks_m, ks_hi, qs_ready = sem("qs_hi"), sem("qs_lo"), sem("ks_m"), sem("ks_hi"), sem("qs_ready")
        vw_hi, vw_lo = sem("vw_hi"), sem("vw_lo")
        u_in, u_sum, u_pool, u_hi, u_lo, u_halo = (sem("u_" + n) for n in ("in", "sum", "pool", "hi", "lo", "halo"))
        gs_hi, gs_lo = sem("gs_hi"), sem("gs_lo")
        c_done, h_add = sem("c_done"), sem("h_add")
        f_ssq, f_std, f_rstd, f_out = sem("f_ssq"), sem("f_std"), sem("f_rstd"), sem("f_out")
        zero_r = sem("zero_r")
        eps_r = sem("eps_r")
        psc_r = sem("psc_r")

        def block_a(h, a):
            return BLOCKS * h + a

        def block_b(h, g, r):
            return BLOCKS * h + A_TILES + GROUP_BLOCKS * g + r

        def block_c(h, tg, e):
            return BLOCKS * h + A_TILES + B_BLOCKS + C_STEPS * tg + e

        def use_a(h, a):
            return USES * h + a

        def use_b(h, g, r):
            return USES * h + A_TILES + GROUP_BLOCKS * g + r

        LAST_BLOCK = BLOCKS * HALVES - 1
        CREDIT = 1

        def settle(eng):
            eng.wait_ge(const_in, 48)

        def z_bank(t):
            return 2 * (t % 3)

        def slot_free(eng, h, pos):
            if not isinstance(pos, int) or pos >= 2:
                eng.wait_ge(pb_done[1], USES * h + pos - 1)
            elif h > 0:
                slot_free_c(eng, h - 1, TG, pos)

        def slot_free_c(eng, h, tg, e):
            if not isinstance(e, int) or e >= 2:
                eng.wait_ge(c_used, (TG * h + tg) * (C_STEPS - 1) + e - 1)
            elif tg == 0:
                eng.wait_ge(pb_done[1], USES * (h + 1) + e - 1)
            elif e == 0:
                eng.wait_ge(c_used, (TG * h + tg) * (C_STEPS - 1))
            else:
                eng.wait_ge(c_done, (TG * h + tg) * 2 * TPG)

        SMALL = 256

        def size_b(r):
            return SMALL if r >= 4 else 1024

        block = ctx.enter_context(nc.Block())

        @block.sync
        def _(sp):
            def load(b, slot, src, size=1024, slot_first=False):
                if not slot_first:
                    sp.wait_ge(w_lo, b - 1)
                sp.dma_start(wraw[:, slot, 0:size], src).then_inc(w_in[slot], 16)

            sp.dma_start(xr[:, 0, :], x[0, 0]).then_inc(x_first[0], 16)
            sp.dma_start(gainn[:, :], gain_n).then_inc(gn_first, 16)
            sp.dma_start(xr[:, 1, :], x[0, 1]).then_inc(x_first[1], 16)
            load(0, 0, wa[0], slot_first=True)
            for t in range(2, 4):
                sp.dma_start(xr[:, t, :], x[0, t]).then_inc(x_first[t], 16)
            load(1, 1, wa[1], slot_first=True)
            for h in range(HALVES):
                if h > 0:
                    for a in range(2):
                        load(block_a(h, a), a, wa[a])
                with sp.Fori(1, A_TILES // 2) as i:
                    for slot in range(2):
                        load(block_a(h, 2 * i + slot), slot, wa[2 * i + slot])
                with sp.Fori(0, NG) as g:
                    for r in range(4):
                        load(block_b(h, g, r), r % 2, wb[g, r])
                    for r in range(2):
                        load(block_b(h, g, 4 + r), r, wp[g, r], SMALL)
                for tg in range(TG):
                    with sp.Fori(0, C_STEPS // 2) as i:
                        for slot in range(2):
                            load(block_c(h, tg, 2 * i + slot), slot, wo[2 * i + slot])

        @block.gpsimd
        def _(pool):
            gp = nc.gpsimd
            gp.dma_start(ident[:, :], ident_d).then_inc(const_in, 16)
            gp.dma_start(cst[:, :], consts).then_inc(const_in, 16)
            gp.dma_start(rotm[:, :, :], rot_meta).then_inc(const_in, 16)
            gp.dma_start(meta_rows[:, :], meta).then_inc(meta_in, 16)
            gp.memset(kh[:, :, :].bitcast(F32), 0.0).then_inc(zero_r, 1)
            gp.memset(kl[:, :, :].bitcast(F32), 0.0).then_inc(s_done, CREDIT)
            gp.memset(vh[:, :, :].bitcast(F32), 0.0).then_inc(o_gate, CREDIT)
            gp.memset(vl[:, :, :].bitcast(F32), 0.0).then_inc(o_done, CREDIT)

            def store_rows(h, tg):
                with pool.Fori(0, TPG) as t:
                    pool.wait_ge(f_out, NTT * h + TPG * tg + t + 1)
                    gp.dma_start(out[h, TPG * tg + t], rows[tg][:, t, :]).then_inc(out_done[tg], 16)

            for h in range(HALVES):
                for t in range(4, NTT):
                    pool.wait_ge(z_t, NTT * h + t - 4 + 1)
                    gp.dma_start(xr[:, t - 4, :], x[h, t]).then_inc(x_in[t - 4], 16)
                if h > 0:
                    pool.wait_ge(c_done, 2 * NTT * h)
                gp.dma_start(cos_t[:, :], rot[h, 0]).then_inc(rot_tab, 16)
                gp.dma_start(sin_t[:, :], rot[h, 1]).then_inc(rot_tab, 16)
                if h > 0:
                    store_rows(h - 1, TG - 1)
                pool.wait_ge(rot_tab, 32 * (h + 1))
                if h == 0:
                    pool.wait_ge(const_in, 48)

                def rotate(r, dst):
                    settle(pool)
                    pool.wait_ge(rot_sw, r + 1)
                    gp.tensor_tensor(rotsrc[:, :], rotsrc[:, :], cos_t[:, :], ALU.mult).then_inc(rot_mul, 1)
                    gp.tensor_tensor(swapped[:, :], swapped[:, :], sin_t[:, :], ALU.mult).then_inc(rot_mul, 1)
                    settle(pool)
                    pool.wait_ge(rot_mul, 2 * r + 2)
                    gp.tensor_tensor(dst, rotsrc[:, :].rearrange("p (c t) -> p c t", t=CH),
                                     swapped[:, :].rearrange("p (c t) -> p c t", t=CH), ALU.add).then_inc(rot_done, 1)

                if h > 0:
                    pool.wait_ge(gs_lo, C_BLOCKS * h)
                rotate((1 + HT) * h, qk[:, :, 0, :])
                if h == 0:
                    pool.wait_ge(km_sw, 1)
                    gp.tensor_tensor(km[:, :], km[:, :], rotm[:, 0, :], ALU.mult).then_inc(km_chain, 1)
                    gp.tensor_tensor(kms[:, :], kms[:, :], rotm[:, 1, :], ALU.mult).then_inc(km_chain, 1)
                    pool.wait_ge(km_chain, 2)
                    gp.tensor_tensor(km[:, :], km[:, :], kms[:, :], ALU.add).then_inc(km_chain, 1)
                    pool.wait_ge(km_chain, 3)
                    pool.wait_ge(zero_r, 1)
                    pool.wait_ge(s_done, 1)
                    for kv in range(2):
                        gp.tensor_tensor(kmm[:, kv, :], km[:, :], cst[:, kv:kv + 1].to_broadcast([P, META]), ALU.mult).then_inc(km_chain, 1)
                    pool.wait_ge(km_chain, 5)
                    gp.tensor_copy(kh[:, 0, META0:KPITCH].rearrange("p (k t) -> p k t", t=META), kmm[:, :, :]).then_inc(km_chain, 1)
                    pool.wait_ge(km_chain, 6)
                    gp.tensor_tensor(kl[:, 0, META0:KPITCH].rearrange("p (k t) -> p k t", t=META), kmm[:, :, :],
                                     kh[:, 0, META0:KPITCH].bitcast(F32).rearrange("p (k t) -> p k t", t=META), ALU.subtract).then_inc(km_done, 1)
                    pool.wait_ge(m_ev, 2)
                    for kv in range(2):
                        last = gp.tensor_tensor(vmm[:, META * kv:META * kv + META], vm[:, :], cst[:, kv:kv + 1].to_broadcast([P, META]), ALU.mult)
                    last.then_inc(vmm_r, 1)
                with pool.Fori(0, HT) as j:
                    rotate((1 + HT) * h + 1 + j, qk[:, :, 1 + j, :])
                pool.wait_ge(rot_done, (1 + HT) * (h + 1))
                gp.memset(ubuf[:, 0:PRE - META], 0.0).then_inc(u_halo, 1)

                with pool.Fori(0, NCH // 2) as pair:
                    for slot in range(2):
                        n = NCH * h + 2 * pair + slot
                        c = 2 * pair + slot
                        keys = slice(CH * slot, CH * slot + CH)
                        settle(pool)
                        pool.wait_ge(s_done, n + CREDIT)
                        gp.tensor_tensor(kmask[:, :, :], qk[:, c, 0:1, :].to_broadcast([P, 2, CH]),
                                         cst[:, 0:2].unsqueeze(2).to_broadcast([P, 2, CH]), ALU.mult).then_inc(ks_m, 1)
                        gp.tensor_copy(qh[:, :].rearrange("p (j t) -> p j t", t=CH), qk[:, c, 1:1 + HT, :]).then_inc(qs_hi, 1)
                        settle(pool)
                        pool.wait_ge(ks_m, n + 1)
                        gp.tensor_copy(kh[:, :, keys], kmask[:, :, :]).then_inc(ks_hi, 1)
                        settle(pool)
                        pool.wait_ge(qs_hi, n + 1)
                        gp.tensor_tensor(ql[:, :].rearrange("p (j t) -> p j t", t=CH), qk[:, c, 1:1 + HT, :],
                                         qh[:, :].bitcast(F32).rearrange("p (j t) -> p j t", t=CH), ALU.subtract).then_inc(qs_lo, 1)
                        settle(pool)
                        pool.wait_ge(ks_hi, n + 1)
                        gp.tensor_tensor(kl[:, :, keys], kmask[:, :, :], kh[:, :, keys].bitcast(F32), ALU.subtract).then_inc(qs_ready, 1)

                pool.wait_ge(vw_lo, NCH * (h + 1))
                pool.wait_ge(pb_done[1], USES * (h + 1))
                pool.wait_ge(o_done, NCH * (h + 1) + CREDIT)
                gp.dma_start(gainf[:, :], gain_f).then_inc(gf_in, 16)
                if h + 1 < HALVES:
                    gp.dma_start(gainn[:, :], gain_n).then_inc(gn_in, 16)
                for tg in range(TG):
                    for t in range(TPG):
                        pool.wait_ge(c_used, (TG * h + tg) * (C_STEPS - 1) + 3 * t + 1)
                        gp.dma_start(rows_in[tg][:, t, :], x[h, TPG * tg + t]).then_inc(res_in, 16)
                        if tg == 0 and h + 1 < HALVES:
                            pool.wait_ge(c_used, (TG * h + tg) * (C_STEPS - 1) + 3 * t + 2)
                            gp.dma_start(xr[:, t, :], x[h + 1, t]).then_inc(x_in[t], 16)
                        if tg == 1:
                            pool.wait_ge(f_out, NTT * h + t + 1)
                            gp.dma_start(out[h, t], rows[0][:, t, :]).then_inc(out_done[0], 16)
            store_rows(HALVES - 1, TG - 1)
            for tg in range(TG):
                pool.wait_ge(out_done[tg], 16 * TPG * HALVES)

        @block.scalar
        def _(act):
            sc = nc.scalar

            def split_hi(h, pos, slot, size=1024):
                if isinstance(pos, tuple):
                    b = block_c(h, *pos)
                    slot_free_c(act, h, *pos)
                else:
                    b = BLOCKS * h + pos
                    slot_free(act, h, pos)
                act.wait_ge(w_in[slot], 8 * (b - slot + 2))
                sc.activation(wh[:, slot, 0:size], wraw[:, slot, 0:size], ACT.Copy).then_inc(w_hi, 1)

            def square(src, junk, acc):
                return sc.activation(junk, src, ACT.Square, scale=1.0 / 32.0, accum_out=acc)

            def z_head(h, t):
                if h == 0 and t < 4:
                    act.wait_ge(x_first[t], 16)
                else:
                    act.wait_ge(x_in[t % 4], 16 * (2 * h + t // 4))
                square(xr[:, t % 4, :], wsum[:, 0:D], ssq[:, t % 4:t % 4 + 1]).then_inc(z_ssq, 1)
                act.wait_ge(z_ssq, NTT * h + t + 1)
                sc.activation(std[:, t % 4:t % 4 + 1], ssq[:, t % 4:t % 4 + 1], ACT.Sqrt, bias=epst).then_inc(z_std, 1)

            def z_tail(h, t):
                act.wait_ge(z_t, NTT * h + t + 1)
                sc.activation(zh[:, t, :, :].rearrange("p k t -> p (k t)"),
                              ps[:, z_bank(t):z_bank(t) + 2, :].rearrange("p b n -> p (b n)"), ACT.Copy).then_inc(z_hi, 1)

            def final_stats(h, t):
                k = NTT * h + t
                act.wait_ge(h_add, 2 * (k + 1))
                square(rows[t // TPG][:, t % TPG, :], wsum[:, 0:D], f_ss[:, t % 4:t % 4 + 1]).then_inc(f_ssq, 1)
                act.wait_ge(f_ssq, k + 1)
                sc.activation(f_sd[:, t % 4:t % 4 + 1], f_ss[:, t % 4:t % 4 + 1], ACT.Sqrt, bias=epst).then_inc(f_std, 1)

            for h in range(HALVES):
                if h == 0:
                    act.wait_ge(eps_r, 1)
                    z_head(0, 0)
                    z_head(0, 1)
                    split_hi(0, 0, 0)
                    z_tail(0, 0)
                    z_head(0, 2)
                    z_tail(0, 1)
                    z_head(0, 3)
                    act.wait_ge(meta_in, 16)
                    square(meta_rows[:, :], wsum[0:META, 0:D], f_ss[0:META, 0:1]).then_inc(zm_step, 1)
                    act.wait_ge(zm_step, 1)
                    sc.activation(f_sd[0:META, 0:1], f_ss[0:META, 0:1], ACT.Sqrt, bias=epst[0:META]).then_inc(zm_step, 1)
                    z_tail(0, 2)
                    z_tail(0, 3)
                    act.wait_ge(zm_step, 5)
                    sc.activation(zmh[:, :, :], ps[:, PB[1], 0:KT * META].rearrange("p (k t) -> p k t", t=META), ACT.Copy).then_inc(zm_step, 1)
                else:
                    for t in range(4):
                        z_tail(h, t)

                def to_rotary(h, a, r, tbs=range(NTB)):
                    for tb in tbs:
                        act.wait_ge(pb_done[tb], use_a(h, a) + 1)
                        if tb == 0 and not (isinstance(r, int) and r == 0):
                            act.wait_ge(rot_done, r)
                        i = sc.activation(rotsrc[:, tb * TB:tb * TB + TB], ps[:, PB[tb], :], ACT.Copy)
                        i.then_inc(rot_in, 1)

                def copy_v(h, tb):
                    act.wait_ge(pb_done[tb], use_a(h, 1) + 1)
                    sc.activation(wsum[:, tb * TB:tb * TB + TB], ps[:, PB[tb], :], ACT.Copy).then_inc(v_in, 1)

                z_head(h, 4)
                z_head(h, 5)
                split_hi(h, 1, 1)
                to_rotary(h, 0, (1 + HT) * h, [0])
                if h > 0:
                    act.wait_ge(out_done[0], 16 * TPG * h)
                z_tail(h, 4)
                z_head(h, 6)
                z_tail(h, 5)
                z_head(h, 7)
                if h > 0:
                    for t in range(TPG, NTT):
                        final_stats(h - 1, t)
                copy_v(h, 0)
                z_tail(h, 6)
                z_tail(h, 7)
                to_rotary(h, 0, (1 + HT) * h, [1])
                if h == 0:
                    act.wait_ge(m_done, 1)
                    sc.activation(km[:, :], ps[:, SPARE, 0:META], ACT.Copy).then_inc(m_ev, 1)
                split_hi(h, 2, 0)
                copy_v(h, 1)
                if h == 0:
                    act.wait_ge(m_done, 2)
                    sc.activation(vm[:, :], ps[:, SPARE, 0:META], ACT.Copy).then_inc(m_ev, 1)
                else:
                    act.wait_ge(f_out, NTT * h)
                act.wait_ge(v_t, h + 1)
                sc.activation(vtok[:, :, :].rearrange("p m f -> p (m f)"), ps[:, 0:2, :].rearrange("p b n -> p (b n)"), ACT.Copy).then_inc(v_tok, 1)
                if h == 0:
                    act.wait_ge(vm_t, 1)
                    sc.activation(vmeta[0:32, :], ps[0:32, SPARE, 0:P], ACT.Copy)
                    sc.activation(vmeta[32:64, :], ps[0:32, SPARE, 0:P], ACT.Copy).then_inc(vm_hi, 1)

                def tanh(use, tb):
                    act.wait_ge(pb_done[tb], use + 1)
                    sc.activation(wsum[:, tb * TB:tb * TB + TB], ps[:, PB[tb], :], ACT.Tanh, scale=0.5).then_inc(tanh_r, 1)

                with act.Fori(0, HT) as j:
                    split_hi(h, 3 + 2 * j, 1)
                    to_rotary(h, 2 + 2 * j, (1 + HT) * h + 1 + j)
                    split_hi(h, 4 + 2 * j, 0)
                    for tb in range(NTB):
                        tanh(use_a(h, 3 + 2 * j), tb)

                with act.Fori(0, NG) as g:
                    for sub in range(4):
                        n = NCH * h + 4 * g + sub
                        split_hi(h, A_TILES + GROUP_BLOCKS * g + sub + 1, (sub + 1) % 2, size_b(sub + 1))
                        act.wait_ge(s_negm, n + 1)
                        for u in range(4):
                            for kv in range(2):
                                sc.activation(probs[:, u, kv * KEYS:kv * KEYS + KEYS], ps[:, u, kv * KEYS:kv * KEYS + KEYS], ACT.Exp,
                                              bias=negm[:, 2 * u + kv:2 * u + kv + 1], scale=SCALE,
                                              accum_out=den[:, 2 * u + kv:2 * u + kv + 1])
                        act.wait_ge(s_sarg, n + 1)
                        sc.activation(esink, sarg, ACT.Exp).then_inc(s_exp, 1)
                        if sub in (1, 2):
                            ut = PT * h + 2 * g + sub - 1
                            act.wait_ge(u_pool, ut + 1)
                            sc.activation(plh[:, sub - 1, :], wsum[:, META:META + TOK], ACT.Copy).then_inc(u_hi, 1)

                        def copy_out(tb):
                            if sub < 2:
                                act.wait_ge(pb_done[tb], use_b(h, g, sub) + 1)
                                if tb == 0:
                                    act.wait_ge(u_halo, (1 + PT) * h + 1 + 2 * g + sub + h)
                                sc.activation(ubuf[:, PRE + tb * TB:PRE + tb * TB + TB], ps[:, PB[tb], :], ACT.Copy).then_inc(u_in, 1)
                            else:
                                if sub == 2 and tb == 0:
                                    act.wait_ge(u_lo, PT * h + 2 * g + 2)
                                tanh(use_b(h, g, sub), tb)

                        copy_out(0)
                        if h == 0 and sub < 2:
                            act.wait_ge(m_done, 2 + 2 * g + sub + 1)
                            sc.activation(ubuf[:, PRE - META:PRE], ps[:, SPARE, 0:META], ACT.Copy).then_inc(m_ev, 1)
                        slot = sub % 2
                        lo_p, hi_p = slot * CH, slot * CH + CH
                        act.wait_ge(o_done, n + CREDIT)
                        sc.activation(vh[lo_p:hi_p, 0:4:3, :], vtok[lo_p:hi_p, 2 * g + sub // 2, :].rearrange("p (k d) -> p k d", k=2),
                                      ACT.Copy).then_inc(vw_hi, 1)
                        act.wait_ge(t_done, n + 1)
                        for kv in range(2):
                            sc.activation(pth[:, kv, :], ps[:, kv, :], ACT.Copy).then_inc(pt_hi, 1)
                        sc.activation(ptm[0:32, :], ps[0:32, 2, :], ACT.Copy).then_inc(pt_hi, 1)
                        sc.activation(ptm[64:96, :], ps[0:32, 2, :], ACT.Copy).then_inc(pt_hi, 1)
                        copy_out(1)
                    split_hi(h, A_TILES + GROUP_BLOCKS * g + 5, 1, SMALL)
                    split_hi(h, A_TILES + GROUP_BLOCKS * g + 6, 0)

                def gated_hi(tg, e, slot):
                    slot_free_c(act, h, tg, e)
                    sc.activation(gsh[:, slot, :], gates[:, e, tg * TB:tg * TB + TB], ACT.Copy).then_inc(gs_hi, 1)

                act.wait_ge(o_gate, NCH * (h + 1) + CREDIT)
                act.wait_ge(pb_free[0], FREES * (h + 1) + CREDIT)
                act.wait_ge(pb_free[1], FREES * (h + 1) + CREDIT)
                gated_hi(0, 0, 0)
                for tg in range(TG):
                    last_group = h + 1 == HALVES and tg + 1 == TG

                    def step(e, slot):
                        split_hi(h, (tg, e + 1), 1 - slot)
                        gated_hi(tg, e + 1, 1 - slot)

                    peeled = 2 if tg == 0 else 8
                    for e in range(peeled):
                        step(e, e % 2)
                        if tg > 0 and e < 4:
                            final_stats(h, e)
                        elif tg > 0 and h + 1 < HALVES:
                            z_head(h + 1, e - 4)
                    with act.Fori(peeled // 2, C_STEPS // 2 - 1) as i:
                        step(2 * i, 0)
                        step(2 * i + 1, 1)
                    step(C_STEPS - 2, 0)
                    if tg + 1 < TG:
                        split_hi(h, (tg + 1, 0), 0)
                        gated_hi(tg + 1, 0, 0)
                    elif not last_group:
                        split_hi(h + 1, 0, 0)
            for t in range(TPG, NTT):
                final_stats(HALVES - 1, t)

        @block.vector
        def _(dve):
            ve = nc.vector

            def split_lo(b, slot, size=1024):
                dve.wait_ge(w_hi, b + 1)
                ve.tensor_tensor(wl[:, slot, 0:size], wraw[:, slot, 0:size], wh[:, slot, 0:size].bitcast(F32), ALU.subtract).then_inc(w_lo, 1)

            def hold():
                ve.memset(small[:, 13:14], 0.0)

            for tb in range(NTB):
                ve.memset(small[:, 14 + tb:15 + tb], 0.0).then_inc(pb_free[tb], CREDIT)
            ve.memset(epst, EPS).then_inc(eps_r, 1)
            dve.wait_ge(const_in, 48)
            ve.tensor_scalar(pgate, pscale, 0.5, None, ALU.mult).then_inc(psc_r, 1)
            ve.tensor_scalar(nsinks, sinks, -1.0, None, ALU.mult).then_inc(psc_r, 1)
            dve.wait_ge(psc_r, 2)

            def z_head(h, t):
                i = t % 4
                dve.wait_ge(z_std, NTT * h + t + 1)
                ve.reciprocal(rstd[:, i:i + 1], std[:, i:i + 1]).then_inc(z_rstd, 1)
                dve.wait_ge(z_rstd, NTT * h + t + 1)
                ve.scalar_tensor_tensor(xr[:, i, :], xr[:, i, :], rstd[:, i:i + 1], gainn[:, :], ALU.mult, ALU.mult).then_inc(z_norm, 1)

            def z_tail(h, t):
                dve.wait_ge(z_hi, NTT * h + t + 1)
                ve.tensor_tensor(zl[:, t, :, :].rearrange("p k t -> p (k t)"),
                                 ps[:, z_bank(t):z_bank(t) + 2, :].rearrange("p b n -> p (b n)"),
                                 zh[:, t, :, :].rearrange("p k t -> p (k t)").bitcast(F32), ALU.subtract).then_inc(z_lo, 1)

            def final_rows(h, t):
                k = NTT * h + t
                i = t % 4
                dve.wait_ge(f_std, k + 1)
                ve.reciprocal(f_rs[:, i:i + 1], f_sd[:, i:i + 1]).then_inc(f_rstd, 1)
                dve.wait_ge(f_rstd, k + 1)
                row = rows[t // TPG][:, t % TPG, :]
                ve.scalar_tensor_tensor(row, row, f_rs[:, i:i + 1], gainf[:, :], ALU.mult, ALU.mult).then_inc(f_out, 1)

            dve.wait_ge(gn_first, 16)
            z_head(0, 0)
            z_head(0, 1)
            split_lo(0, 0)
            z_tail(0, 0)
            z_head(0, 2)
            z_tail(0, 1)
            z_head(0, 3)
            dve.wait_ge(zm_step, 2)
            ve.reciprocal(f_rs[0:META, 0:1], f_sd[0:META, 0:1]).then_inc(zm_step, 1)
            dve.wait_ge(zm_step, 3)
            ve.scalar_tensor_tensor(meta_rows[:, :], meta_rows[:, :], f_rs[0:META, 0:1], gainn[0:META, :], ALU.mult, ALU.mult).then_inc(zm_step, 1)
            z_tail(0, 2)
            z_tail(0, 3)
            dve.wait_ge(zm_step, 6)
            ve.tensor_tensor(zml[:, :, :], ps[:, PB[1], 0:KT * META].rearrange("p (k t) -> p k t", t=META), zmh[:, :, :].bitcast(F32), ALU.subtract).then_inc(zm_step, 1)

            for h in range(HALVES):
                if h > 0:
                    for t in range(4):
                        z_tail(h, t)

                SWAP = [(i + 8) % 16 if i < 16 else i for i in range(32)]

                def swap(r):
                    dve.wait_ge(rot_in, 2 * r + 2)
                    hold()
                    ve.stream_shuffle(swapped[:, :], rotsrc[:, :], SWAP).then_inc(rot_sw, 1)

                def silu(dst, use, count, tb):
                    dve.wait_ge(tanh_r, count)
                    ve.scalar_tensor_tensor(dst, wsum[:, tb * TB:tb * TB + TB], 1.0, ps[:, PB[tb], :], ALU.add, ALU.mult).then_inc(pb_free[tb], 1)

                z_head(h, 4)
                z_head(h, 5)
                split_lo(block_a(h, 1), 1)
                z_tail(h, 4)
                z_head(h, 6)
                z_tail(h, 5)
                z_head(h, 7)
                z_tail(h, 6)
                z_tail(h, 7)
                split_lo(block_a(h, 2), 0)
                swap((1 + HT) * h)
                if h > 0:
                    for t in range(TPG, NTT):
                        final_rows(h - 1, t)
                if h == 0:
                    dve.wait_ge(m_ev, 1)
                    ve.stream_shuffle(kms[:, :], km[:, :], SWAP).then_inc(km_sw, 1)
                if h == 0:
                    dve.wait_ge(vm_hi, 1)
                    ve.tensor_tensor(vmeta[64:96, :], ps[0:32, SPARE, 0:P], vmeta[0:32, :].bitcast(F32), ALU.subtract).then_inc(vm_done, 1)
                else:
                    dve.wait_ge(out_done[1], 16 * TPG * h)
                with dve.Fori(0, HT) as j:
                    split_lo(block_a(h, 3 + 2 * j), 1)
                    swap((1 + HT) * h + 1 + j)
                    split_lo(block_a(h, 4 + 2 * j), 0)
                    for tb in range(NTB):
                        silu(gates[:, j, tb * TB:tb * TB + TB], use_a(h, 3 + 2 * j), (2 * HT + 2 * PT) * h + 2 * j + tb + 1, tb)

                with dve.Fori(0, NG) as g:
                    for sub in range(4):
                        n = NCH * h + 4 * g + sub
                        scores = ps[:, 0:4, 0:2 * KEYS].rearrange("p u (k s) -> p u k s", k=2)
                        dve.wait_ge(s_done, n + 1 + CREDIT)
                        if h == 0 and sub == 0:
                            for kv in range(2):
                                empty = ps[:, 0:4, kv * KPITCH + CH:kv * KPITCH + 2 * CH]
                                i = ve.tensor_scalar(empty, empty, cst[:, bass.ds(6 + g, 1)], None, ALU.add)
                                i.then_inc(s_mask, 1)
                            dve.wait_ge(s_mask, 2 * (g + 1))
                        ve.tensor_reduce(mx, scores, AXX, ALU.max).then_inc(s_max, 1)
                        dve.wait_ge(s_max, n + 1)
                        ve.scalar_tensor_tensor(negm, mx, -SCALE, nsinks, ALU.mult, ALU.min).then_inc(s_negm, 1)
                        dve.wait_ge(s_negm, n + 1)
                        ve.tensor_tensor(sarg, negm, sinks, ALU.add).then_inc(s_sarg, 1)
                        if sub in (1, 2):
                            ut = PT * h + 2 * g + sub - 1
                            dve.wait_ge(u_in, 2 * ut + 2)
                            if h == 0:
                                dve.wait_ge(m_ev, 2 + ut + 1)
                            hold()
                            ve.tensor_tensor_scan(wsum[:, :], ubuf[:, META:PRE + TOK], ubuf[:, bass.ds(META - (2 << g), META + TOK)], 0.0,
                                                  ALU.add, ALU.subtract).then_inc(u_sum, 1)
                            dve.wait_ge(u_sum, ut + 1)
                            ve.scalar_tensor_tensor(wsum[:, META:META + TOK], wsum[:, META:META + TOK], cst[:, bass.ds(2 + g, 1)],
                                                    ubuf[:, PRE:PRE + TOK], ALU.mult, ALU.subtract).then_inc(u_pool, 1)
                            if h == 0:
                                ve.tensor_copy(halo[:, 2 * g + sub - 1, :], ubuf[:, TOK + PRE - META:TOK + PRE]).then_inc(u_halo, 1)
                        if h > 0 and sub < 2:
                            dve.wait_ge(u_halo, 1 + PT + 1 + 2 * g + sub)
                            ve.tensor_copy(ubuf[:, PRE - META:PRE], halo[:, 2 * g + sub, :]).then_inc(u_halo, 1)
                        split_lo(block_b(h, g, sub + 1), (sub + 1) % 2, size_b(sub + 1))
                        dve.wait_ge(s_exp, n + 1)
                        ve.tensor_tensor(dsum, den, esink, ALU.add).then_inc(d_sum, 1)
                        dve.wait_ge(d_sum, n + 1)
                        ve.reciprocal(rden, dsum).then_inc(d_rcp, 1)
                        dve.wait_ge(d_rcp, n + 1)
                        pr = probs[:, :, :].rearrange("p u (k s) -> p (u k) s", k=2)
                        ve.tensor_tensor(pr, pr, rden.unsqueeze(2).to_broadcast([P, 8, KEYS]), ALU.mult).then_inc(p_ready, 1)
                        if sub in (1, 2):
                            dve.wait_ge(u_hi, ut + 1)
                            ve.tensor_tensor(pll[:, sub - 1, :], wsum[:, META:META + TOK], plh[:, sub - 1, :].bitcast(F32), ALU.subtract).then_inc(u_lo, 1)

                        def gate_tile(tb):
                            if sub >= 2:
                                silu(gates[:, HT + 2 * g + sub - 2, tb * TB:tb * TB + TB], None,
                                     (2 * HT + 2 * PT) * h + 2 * HT + 2 * (2 * g + sub - 2) + tb + 1, tb)

                        gate_tile(0)
                        slot = sub % 2
                        lo_p, hi_p = slot * CH, slot * CH + CH
                        dve.wait_ge(vw_hi, n + 1)
                        ve.tensor_tensor(vl[lo_p:hi_p, 0:4:3, :], vtok[lo_p:hi_p, 2 * g + sub // 2, :].rearrange("p (k d) -> p k d", k=2),
                                         vh[lo_p:hi_p, 0:4:3, :].bitcast(F32), ALU.subtract).then_inc(vw_lo, 1)
                        for kv in range(2):
                            dve.wait_ge(pt_hi, 4 * n + kv + 1)
                            ve.tensor_tensor(ptl[:, kv, :], ps[:, kv, :], pth[:, kv, :].bitcast(F32), ALU.subtract)
                        dve.wait_ge(pt_hi, 4 * n + 4)
                        ve.tensor_tensor(ptm[32:64, :], ps[0:32, 2, :], ptm[0:32, :].bitcast(F32), ALU.subtract).then_inc(pt_lo, 1)
                        gate_tile(1)
                        dve.wait_ge(o_done, n + 1 + CREDIT)
                        gslice = gates[:, 0:HT, bass.ds((4 * g + sub) * CH, CH)]
                        ve.scalar_tensor_tensor(gslice, ps[:, OB, :].rearrange("p (j t) -> p j t", t=CH), 0.5, gslice, ALU.mult, ALU.mult).then_inc(o_gate, 1)
                    split_lo(block_b(h, g, 5), 1, SMALL)
                    for dt in range(2):
                        if dt == 1:
                            split_lo(block_b(h, g, 6), 0)
                        for tb in range(NTB):
                            dve.wait_ge(pb_done[tb], use_b(h, g, 4 + dt) + 1)
                            gt = gates[:, HT + 2 * g + dt, tb * TB:tb * TB + TB]
                            ve.scalar_tensor_tensor(gt, ps[:, PB[tb], :], stat[:, bass.ds(56 + 2 * g + dt, 1)], gt, ALU.mult, ALU.mult).then_inc(pb_free[tb], 1)

                def gated_lo(tg, e, slot):
                    b = C_BLOCKS * h + C_STEPS * tg + e
                    dve.wait_ge(gs_hi, b + 1)
                    ve.tensor_tensor(gsl[:, slot, :], gates[:, e, tg * TB:tg * TB + TB], gsh[:, slot, :].bitcast(F32), ALU.subtract).then_inc(gs_lo, 1)

                def add_rows(tg, t):
                    for dh in range(2):
                        k = NTT * h + tg * TPG + t
                        dve.wait_ge(c_done, 2 * k + dh + 1)
                        part = slice(dh * TB, dh * TB + TB)
                        ve.tensor_tensor(rows[tg][:, t, part], ps[:, 2 * t + dh, :], rows_in[tg][:, t, part], ALU.add).then_inc(h_add, 1)

                gated_lo(0, 0, 0)
                for tg in range(TG):
                    last_group = h + 1 == HALVES and tg + 1 == TG

                    def step(e, slot):
                        split_lo(block_c(h, tg, e) + 1, 1 - slot)
                        gated_lo(tg, e + 1, 1 - slot)

                    peeled = 2 if tg == 0 else 8
                    for e in range(peeled):
                        step(e, e % 2)
                        if tg > 0 and e == 0:
                            dve.wait_ge(gf_in, 16 * (h + 1))
                        if tg > 0 and e == 4 and h + 1 < HALVES:
                            dve.wait_ge(gn_in, 16 * (h + 1))
                        if tg > 0 and e < 4:
                            final_rows(h, e)
                        elif tg > 0 and h + 1 < HALVES:
                            z_head(h + 1, e - 4)
                    with dve.Fori(peeled // 2, C_STEPS // 2 - 1) as i:
                        step(2 * i, 0)
                        step(2 * i + 1, 1)
                    step(C_STEPS - 2, 0)
                    if not last_group:
                        split_lo(block_c(h, tg, C_STEPS - 1) + 1, 0)
                    if tg + 1 < TG:
                        gated_lo(tg + 1, 0, 0)
                    dve.wait_ge(res_in, 16 * (NTT * h + TPG * (tg + 1)))
                    for t in range(TPG):
                        add_rows(tg, t)
                        if last_group and t > 0:
                            final_rows(h, TPG + t - 1)
            final_rows(HALVES - 1, NTT - 1)

        @block.tensor
        def _(pe):
            te = nc.tensor

            def rhs_z(z, tb, k):
                return z[:, tb * (TB // P):(tb + 1) * (TB // P), k, :]

            def project(slot, tb, k0, k1):
                for k in range(k0, k1):
                    w_h, w_l = wh[:, slot, k * P:k * P + P], wl[:, slot, k * P:k * P + P]
                    te.matmul(ps[:, PB[tb], :], w_h, rhs_z(zh, tb, k), start=k == 0, stop=False)
                    te.matmul(ps[:, PB[tb], :], w_h, rhs_z(zl, tb, k), start=False, stop=False)
                    last = te.matmul(ps[:, PB[tb], :], w_l, rhs_z(zh, tb, k), start=False, stop=k == KT - 1)
                if k1 == KT:
                    last.then_inc(pb_done[tb], 1)
                return last

            def project_meta(slot):
                for k in range(KT):
                    w_h, w_l = wh[:, slot, k * P:k * P + P], wl[:, slot, k * P:k * P + P]
                    te.matmul(ps[:, SPARE, 0:META], w_h, zmh[:, k, :], start=k == 0, stop=False)
                    te.matmul(ps[:, SPARE, 0:META], w_h, zml[:, k, :], start=False, stop=False)
                    last = te.matmul(ps[:, SPARE, 0:META], w_l, zmh[:, k, :], start=False, stop=k == KT - 1)
                last.then_inc(m_done, 1)
                return last

            def z_transpose(h, t):
                pe.wait_ge(z_norm, NTT * h + t + 1)
                if t >= 3:
                    pe.wait_ge(z_lo, NTT * h + t - 2)
                elif h > 0:
                    pe.wait_ge(h_add, 2 * (NTT * h - TPG + t + 1))
                for k in range(KT):
                    last = te.transpose(ps[:, z_bank(t) + k // 4, (k % 4) * P:(k % 4) * P + P], xr[:, t % 4, k * P:k * P + P], ident[:, :])
                last.then_inc(z_t, 1)

            pe.wait_ge(const_in, 48)
            for h in range(HALVES):
                for t in range(4):
                    z_transpose(h, t)
                if h == 0:
                    pe.wait_ge(zm_step, 4)
                    for k in range(KT):
                        last = te.transpose(ps[:, PB[1], k * META:k * META + META], meta_rows[:, k * P:k * P + P], ident[0:META, 0:META])
                    last.then_inc(zm_step, 1)
                else:
                    pe.wait_ge(h_add, 2 * NTT * h)

                def tile_a(a, slot, bank_free):
                    pe.wait_ge(w_lo, block_a(h, a) + 1)
                    for tb in range(NTB):
                        bank_free(tb)
                        project(slot, tb, 0, KT)

                pe.wait_ge(w_lo, block_a(h, 0) + 1)
                pe.wait_ge(z_lo, NTT * h + 4)
                project(0, 0, 0, KT)
                z_transpose(h, 4)
                z_transpose(h, 5)
                pe.wait_ge(w_lo, block_a(h, 1) + 1)
                pe.wait_ge(rot_in, 2 * (1 + HT) * h + 1)
                project(1, 0, 0, KT)
                z_transpose(h, 6)
                z_transpose(h, 7)
                pe.wait_ge(z_lo, NTT * (h + 1))
                if h == 0:
                    pe.wait_ge(zm_step, 7)
                project(0, 1, 0, KT)
                if h == 0:
                    project_meta(0)
                pe.wait_ge(rot_in, 2 * (1 + HT) * h + 2)
                project(1, 1, 0, KT)
                if h == 0:
                    pe.wait_ge(m_ev, 1)
                    project_meta(1)
                pe.wait_ge(v_in, 2 * (h + 1))
                for m in range(NTT):
                    last = te.transpose(ps[:, m // 4, (m % 4) * P:(m % 4) * P + P], wsum[:, m * P:m * P + P], ident[:, :])
                last.then_inc(v_t, 1)
                if h == 0:
                    pe.wait_ge(vmm_r, 1)
                    te.transpose(ps[0:32, SPARE, 0:P], vmm[:, :], ident[:, :]).then_inc(vm_t, 1)
                with pe.Fori(0, HT) as j:
                    tile_a(2 + 2 * j, 0, lambda tb: pe.wait_ge(pb_free[tb], FREES * h + j + CREDIT))
                    tile_a(3 + 2 * j, 1, lambda tb: pe.wait_ge(rot_in, 2 * ((1 + HT) * h + 1 + j) + tb + 1))

                if h == 0:
                    pe.wait_ge(km_done, 1)
                    pe.wait_ge(vm_done, 1)
                with pe.Fori(0, NG) as g:
                    for sub in range(4):
                        n = NCH * h + 4 * g + sub
                        slot = sub % 2
                        pe.wait_ge(qs_ready, n + 1)
                        for u in range(4):
                            q_h, q_l = qh[:, u * P:u * P + P], ql[:, u * P:u * P + P]
                            so = ps[:, u, 0:2 * KEYS]
                            k_h, k_l = (w[:, :, :].rearrange("p k s -> p (k s)")[:, 0:2 * KEYS] for w in (kh, kl))
                            te.matmul(so, q_h, k_h, start=True, stop=False)
                            te.matmul(so, q_h, k_l, start=False, stop=False)
                            last = te.matmul(so, q_l, k_h, start=False, stop=True)
                        last.then_inc(s_done, 1)
                        pe.wait_ge(w_lo, block_b(h, g, sub) + 1)
                        ut = PT * h + 2 * g + sub

                        def bank_free(tb):
                            if sub in (1, 2):
                                pe.wait_ge(u_in, 2 * (ut - 1) + tb + 1)
                            else:
                                pe.wait_ge(pb_free[tb], FREES * h + HT + 4 * g + sub // 3 + CREDIT)

                        bank_free(0)
                        project(slot, 0, 0, KT)
                        if h == 0 and sub < 2:
                            pe.wait_ge(m_ev, 2 + 2 * g + sub)
                            project_meta(slot)
                        bank_free(1)
                        project(slot, 1, 0, 3)
                        pe.wait_ge(p_ready, n + 1)
                        for kv in range(2):
                            for u in range(4):
                                te.transpose(ps[:, kv, u * P:u * P + P], probs[:, u, kv * KPITCH:kv * KPITCH + 2 * CH], ident[:, :])
                        for u in range(4):
                            last = te.transpose(ps[0:32, 2, u * P:u * P + P], probs[:, u, META0:KPITCH], ident[:, :])
                        last.then_inc(t_done, 1)
                        project(slot, 1, 3, KT)
                        pe.wait_ge(pt_lo, n + 1)
                        pe.wait_ge(vw_lo, n + 1)
                        pe.wait_ge(o_gate, n + CREDIT)
                        ob = ps[:, OB, :]
                        for kv in range(2):
                            v_h = vh[:, 2 * kv:2 * kv + 2, :].rearrange("p a d -> p (a d)")
                            v_l = vl[:, 2 * kv:2 * kv + 2, :].rearrange("p a d -> p (a d)")
                            te.matmul(ob, v_h, pth[:, kv, :], start=kv == 0, stop=False)
                            te.matmul(ob, v_h, ptl[:, kv, :], start=False, stop=False)
                            te.matmul(ob, v_l, pth[:, kv, :], start=False, stop=False)
                        te.matmul(ob, vmeta[0:96, :], ptm[0:96, :], start=False, stop=True).then_inc(o_done, 1)
                    for dt in range(2):
                        pe.wait_ge(w_lo, block_b(h, g, 4 + dt) + 1)
                        pe.wait_ge(u_lo, PT * h + 2 * g + 2)
                        for tb in range(NTB):
                            pe.wait_ge(pb_free[tb], FREES * h + HT + 4 * g + 2 + dt + CREDIT)
                            mo = ps[:, PB[tb], :]
                            for ct in range(2):
                                m_h, m_l = wh[:, dt, ct * P:ct * P + P], wl[:, dt, ct * P:ct * P + P]
                                te.matmul(mo, m_h, plh[:, ct, tb * TB:tb * TB + TB], start=ct == 0, stop=False)
                                te.matmul(mo, m_h, pll[:, ct, tb * TB:tb * TB + TB], start=False, stop=False)
                                last = te.matmul(mo, m_l, plh[:, ct, tb * TB:tb * TB + TB], start=False, stop=ct == 1)
                            last.then_inc(pb_done[tb], 1)

                for tg in range(TG):
                    def step(e, slot, first=False, final=False):
                        pe.wait_ge(w_lo, block_c(h, tg, e) + 1)
                        pe.wait_ge(gs_lo, C_BLOCKS * h + C_STEPS * tg + e + 1)
                        for t in range(TPG):
                            g_h, g_l = gsh[:, slot, t * P:t * P + P], gsl[:, slot, t * P:t * P + P]
                            for dh in range(2):
                                if first and tg > 0:
                                    pe.wait_ge(h_add, 2 * (NTT * h + (tg - 1) * TPG + t) + dh + 1)
                                w_h, w_l = wh[:, slot, dh * TB:dh * TB + TB], wl[:, slot, dh * TB:dh * TB + TB]
                                co = ps[:, 2 * t + dh, :]
                                te.matmul(co, g_h, w_h, start=first, stop=False)
                                te.matmul(co, g_h, w_l, start=False, stop=False)
                                last = te.matmul(co, g_l, w_h, start=False, stop=final)
                                if final:
                                    last.then_inc(c_done, 1)
                        if not final:
                            last.then_inc(c_used, 1)

                    if tg == 0:
                        for tb in range(NTB):
                            pe.wait_ge(pb_free[tb], FREES * (h + 1) + CREDIT)
                        pe.wait_ge(o_gate, NCH * (h + 1) + CREDIT)
                    step(0, 0, first=True)
                    step(1, 1)
                    with pe.Fori(1, C_STEPS // 2 - 1) as i:
                        step(2 * i, 0)
                        step(2 * i + 1, 1)
                    step(C_STEPS - 2, 0)
                    step(C_STEPS - 1, 1, final=True)


_INS = ["x", "meta", "wa", "wb", "wp", "wo", "gain_n", "gain_f", "consts", "ident", "rot", "rot_meta"]


def rotary_tables():
    half = HD // 4 // 2
    inv = (np.float32(500000.0) ** (-np.arange(half, dtype=np.float32) * np.float32(2.0 / (HD // 4)))).astype(np.float32)
    ang = np.arange(META + SEQ, dtype=np.float32)[None, :] * inv[:, None]
    cos, sin = np.cos(ang).astype(np.float32), np.sin(ang).astype(np.float32)
    c = np.ones((HD, META + SEQ), np.float32)
    s = np.zeros((HD, META + SEQ), np.float32)
    c[0:half], c[half:2 * half] = cos, cos
    s[0:half], s[half:2 * half] = -sin, sin
    return np.concatenate([c, c]), np.concatenate([s, s])


def kernel(x, meta_tokens, norm_gain, w_in, attn_sinks, w_pool, pool_scale, w_out, final_norm_gain):
    import concourse.bacc as bacc
    from concourse.bass_utils import run_bass_kernel_spmd

    w = np.asarray(w_in)[0]
    pairs = [np.r_[j * HD:(j + 1) * HD, (HT + j) * HD:(HT + j + 1) * HD] for j in range(HT)]
    q0, k0, v0, g0 = 0, HT * P, HT * P + P, HT * P + 2 * P
    u0 = g0 + HT * P
    p0 = u0 + PT * P

    def tiles(cols):
        t = w[:, np.stack(cols)]
        return np.ascontiguousarray(t.reshape(KT, P, len(cols), P).transpose(2, 1, 0, 3).reshape(len(cols), P, KT * P))

    cols = [np.arange(k0, k0 + P), np.arange(v0, v0 + P)]
    for j in range(HT):
        cols += [q0 + pairs[j], g0 + pairs[j]]
    wa = tiles(cols)
    cols = []
    for g in range(NG):
        for first in (u0, p0):
            cols += [np.arange(first + (2 * g + i) * P, first + (2 * g + i + 1) * P) for i in range(2)]
    wb = tiles(cols).reshape(NG, 4, P, KT * P)
    wp = np.ascontiguousarray(np.asarray(w_pool)[0].reshape(NG, 2, P, 2, P).transpose(0, 3, 2, 1, 4).reshape(NG, 2, P, 2 * P))
    rows = np.concatenate(pairs + [HT * P + np.arange(PT * P)])
    wo = np.ascontiguousarray(np.asarray(w_out)[0][rows].reshape(C_STEPS, P, D))

    consts = np.zeros((P, 32), np.float32)
    consts[:HD, 0] = 1.0
    consts[HD:, 1] = 1.0
    consts[:, 2:6] = [0.5, 0.25, 0.125, 0.0625]
    consts[:, 6] = -1e30
    sinks = np.asarray(attn_sinks)[0]
    for u in range(4):
        for kv in range(2):
            for i in range(2):
                consts[i * CH:(i + 1) * CH, 10 + 2 * u + kv] = sinks[kv * 8 + 2 * u + i]
    consts[:, 18:26] = np.asarray(pool_scale)[0].reshape(PT, P).T
    cos, sin = rotary_tables()
    rot = np.stack([np.stack([t[:, META + h * TOK:META + (h + 1) * TOK] for t in (cos, sin)]) for h in range(HALVES)])
    rot_meta = np.stack([cos[:, :META], sin[:, :META]], axis=1)

    arrays = {
        "x": np.asarray(x)[0].reshape(HALVES, NTT, P, D),
        "meta": np.asarray(meta_tokens),
        "wa": wa, "wb": wb, "wp": wp, "wo": wo,
        "gain_n": np.broadcast_to(np.asarray(norm_gain)[0], (P, D)),
        "gain_f": np.broadcast_to(np.asarray(final_norm_gain), (P, D)),
        "consts": consts, "ident": np.eye(P, dtype=np.float32), "rot": rot, "rot_meta": rot_meta,
    }
    nc = bacc.Bacc("TRN2", target_bir_lowering=False, num_devices=1)
    ins, args = {}, []
    for name in _INS:
        a = np.ascontiguousarray(arrays[name])
        ins[f"in_{name}"] = a
        args.append(nc.dram_tensor(f"in_{name}", a.shape, mybir.dt.from_np(a.dtype), kind="ExternalInput").ap())
    out = nc.dram_tensor("out_y", (HALVES, NTT, P, D), F32, kind="ExternalOutput").ap()
    build(nc, *args, out)
    r = run_bass_kernel_spmd(nc, [ins], core_ids=[0])
    return r.results[0]["out_y"].reshape(1, SEQ, D)
```

```python
from contextlib import ExitStack

import numpy as np

import concourse.bass as bass
from concourse import mybir

F32 = mybir.dt.float32
F32R = mybir.dt.float32r
ACT = mybir.ActivationFunctionType
ALU = mybir.AluOpType
AXX = mybir.AxisListType.X

P = 128
D = 1024
KT = D // P
SEQ = 2048
META = 16
CH = 64
HD = 64
HALVES = 2
TOK = SEQ // HALVES
NTT = TOK // P
NCH = TOK // CH
TB = 512
NTB = TOK // TB
HT = 8
PT = 8
NG = 4
KEYS = META + 2 * CH
KPITCH = KEYS + META
META0 = 2 * CH
EPS = 1e-6
SOFTMAX_STEPS = 3
WARM = 20
SCALE = HD ** -0.5
PRE = 32

A_TILES = 2 + 2 * HT
GROUP_BLOCKS = 6
B_BLOCKS = NG * GROUP_BLOCKS
C_STEPS = HT + PT
TG = 2
TPG = NTT // TG
C_BLOCKS = TG * C_STEPS
BLOCKS = A_TILES + B_BLOCKS + C_BLOCKS
USES = A_TILES + B_BLOCKS
FREES = HT + 4 * NG


def build(nc, x, meta, wa, wb, wp, wo, gain_n, gain_f, consts, ident_d, rot, rot_meta, out):
    ctx = ExitStack()
    with ctx:
        base = 16512
        arena = ctx.enter_context(nc.sbuf_tensor("arena", [P, (229344 - base - 64) // 4], F32))
        cursor = [base]

        def at(offset, name, shape, dt=F32):
            return nc.alloc_sbuf_tensor_at(name, shape, dt, offset=offset)

        def place(name, shape, dt=F32):
            size = 4 * int(np.prod(shape[1:]))
            offset = cursor[0]
            cursor[0] += (size + 31) // 32 * 32
            return at(offset, name, shape, dt), offset

        zh, zh_at = place("zh", [P, NTT, KT, P], F32R)
        zl, zl_at = place("zl", [P, NTT, KT, P], F32R)
        rows_in = [at(offset + 4 * TPG * D, name, [P, TPG, D]) for name, offset in (("rows0", zh_at), ("rows1", zl_at))]
        gates, g_at = place("gates", [P, HT, TOK])
        rows = [rows_in[0], at(g_at, "rows1_out", [P, TPG, D])]
        gainf1 = at(g_at + 4 * TOK * (HT - 1), "gainf1", [P, D])
        meta_rows = at(g_at, "meta_rows", [META, D])
        qk, qk_at = place("qk", [P, NCH, 1 + HT, CH])
        gates = at(g_at, "gates_all", [P, HT + PT, TOK])
        wraw, _ = place("wraw", [P, 2, 1024])
        wsplit, _ = place("wsplit", [P, 2, 2, 1024], F32R)
        plh, pool_at = place("plh", [P, 2, TOK], F32R)
        pll, _ = place("pll", [P, 2, TOK], F32R)
        cos_t = at(pool_at, "cos_t", [P, TOK])
        sin_t = at(pool_at + 4096, "sin_t", [P, TOK])
        gainn = at(pool_at + 8192, "gainn", [P, D])
        swapped = at(pool_at + 12288, "swapped", [P, TOK])
        junk = at(pool_at + 12288, "junk", [P, D])
        r_at = cursor[0]
        pth, pth_at = place("pth", [P, 2, TB], F32R)
        ptl, _ = place("ptl", [P, 2, TB], F32R)
        probs = at(pth_at, "probs", [P, 4, 2 * KEYS])
        ptm, _ = place("ptm", [P, TB], F32R)
        qh, _ = place("qh", [P, HT * CH], F32R)
        ql, _ = place("ql", [P, HT * CH], F32R)
        kmask, _ = place("kmask", [P, 2, CH])
        km, _ = place("km", [P, META])
        kms, _ = place("kms", [P, META])
        kmm, _ = place("kmm", [P, 2, META])
        vm, _ = place("vm", [P, META])
        vmm, _ = place("vmm", [P, 2 * META])
        mprod, _ = place("mprod", [P, 2 * P])
        assert cursor[0] <= r_at + 4 * 4096
        xr = at(r_at, "xr", [P, 4, D])
        cursor[0] = r_at + 4 * 4096
        ubuf, u_at = place("ubuf", [P, PRE + TOK])
        rotsrc = at(u_at, "rotsrc", [P, TOK])
        gsh = at(u_at, "gsh", [P, 2, TB], F32R)
        wsum, wsum_at = place("wsum", [P, META + TOK])
        gsl = at(wsum_at, "gsl", [P, 2, TB], F32R)
        vtok, vtok_at = place("vtok", [P, NTT, P])
        gainf = at(vtok_at, "gainf", [P, D])
        kh, _ = place("kh", [P, 2, KPITCH], F32R)
        kl, _ = place("kl", [P, 2, KPITCH], F32R)
        vh, _ = place("vh", [P, 4, HD], F32R)
        vl, _ = place("vl", [P, 4, HD], F32R)
        vmeta, _ = place("vmeta", [P, P], F32R)
        ident, _ = place("ident", [P, P])
        halo, _ = place("halo", [P, PT, META])
        zm, _ = place("zm", [P, KT, 2, META], F32R)
        cst, _ = place("cst", [P, 32])
        rotm, _ = place("rotm", [P, 2, META])
        stat, _ = place("stat", [P, 72])
        small, _ = place("small", [P, 16])
        assert cursor[0] <= 229344, cursor[0]
        sinks, pscale = cst[:, 10:18], cst[:, 18:26]
        wh, wl = wsplit[:, :, 0, :], wsplit[:, :, 1, :]
        mx, negm, sarg, esink = (stat[:, 8 * i:8 * i + 8] for i in range(4))
        den, dsum, rden, pgate = (stat[:, 8 * i:8 * i + 8] for i in range(4, 8))
        f_ss, f_sd, f_rs = (stat[:, 8 * i:8 * i + 4] for i in range(3))
        ssq, std, rstd = small[:, 0:4], small[:, 4:8], small[:, 8:12]
        epst = small[:, 12:13]
        nsinks = stat[:, 64:72]

        ps = ctx.enter_context(nc.psum_tensor("ps", [P, 8, TB], F32))
        OB, SPARE, PB = 4, 5, (6, 7)

        def sem(name):
            return ctx.enter_context(nc.semaphore(name))

        ident_in = sem("ident_in")
        const_in = sem("const_in")
        meta_in = sem("meta_in")
        gn_first, gn_in = sem("gn_first"), sem("gn_in")
        gf_in = sem("gf_in")
        rot_tab = sem("rot_tab")
        x_first = [sem(f"x_first{i}") for i in range(4)]
        x_in = [sem(f"x_in{i}") for i in range(4)]
        res_in = sem("res_in")
        w_in = [sem(f"w_in{i}") for i in range(2)]
        out_last = sem("out_last")
        out_done = [sem(f"out_done{i}") for i in range(TG)]
        zm_step = sem("zm_step")
        z_ssq, z_std, z_rstd, z_norm, z_t, z_hi, z_lo = (sem("z_" + n) for n in ("ssq", "std", "rstd", "norm", "t", "hi", "lo"))
        w_hi, w_lo, c_used = sem("w_hi"), sem("w_lo"), sem("c_used")
        pb_done = [sem(f"pb_done{i}") for i in range(2)]
        pb_free = [sem(f"pb_free{i}") for i in range(2)]
        rot_in, rot_sw, rot_sin, rot_cos, rot_done = (sem("rot_" + n) for n in ("in", "sw", "sin", "cos", "done"))
        v_in, v_t, v_tok = sem("v_in"), sem("v_t"), sem("v_tok")
        vmm_r, vm_t, vm_hi, vm_done = sem("vmm_r"), sem("vm_t"), sem("vm_hi"), sem("vm_done")
        m_prod, m_sb, m_done, m_ev = sem("m_prod"), sem("m_sb"), sem("m_done"), sem("m_ev")
        km_sw, km_chain, km_done = sem("km_sw"), sem("km_chain"), sem("km_done")
        tanh_r = sem("tanh_r")
        s_done, s_mask, s_max, s_negm, s_sarg, s_exp = (sem("s_" + n) for n in ("done", "mask", "max", "negm", "sarg", "exp"))
        d_sum, d_rcp, p_ready, t_done = sem("d_sum"), sem("d_rcp"), sem("p_ready"), sem("t_done")
        pt_hi, pt_lo = sem("pt_hi"), sem("pt_lo")
        o_done, o_gate = sem("o_done"), sem("o_gate")
        qs_hi, qs_lo, ks_m, ks_hi, qs_ready = sem("qs_hi"), sem("qs_lo"), sem("ks_m"), sem("ks_hi"), sem("qs_ready")
        vw_hi, vw_lo = sem("vw_hi"), sem("vw_lo")
        u_in, u_sum, u_pool, u_hi, u_lo, u_halo = (sem("u_" + n) for n in ("in", "sum", "pool", "hi", "lo", "halo"))
        gs_hi, gs_lo, gs_first = sem("gs_hi"), sem("gs_lo"), sem("gs_first")
        c_done, h_add = sem("c_done"), sem("h_add")
        f_ssq, f_std, f_rstd, f_out = sem("f_ssq"), sem("f_std"), sem("f_rstd"), sem("f_out")
        zero_r = sem("zero_r")
        eps_r = sem("eps_r")
        psc_r = sem("psc_r")

        def block_a(h, a):
            return BLOCKS * h + a

        def block_b(h, g, r):
            return BLOCKS * h + A_TILES + GROUP_BLOCKS * g + r

        def block_c(h, tg, e):
            return BLOCKS * h + A_TILES + B_BLOCKS + C_STEPS * tg + e

        def use_a(h, a):
            return USES * h + a

        def use_b(h, g, r):
            return USES * h + A_TILES + GROUP_BLOCKS * g + r

        LAST_BLOCK = BLOCKS * HALVES - 1
        CREDIT = 1

        def settle(eng):
            eng.wait_ge(const_in, 32)

        def z_bank(t):
            return PB[0] if t == 3 else 2 * (t % 3)

        def slot_free(eng, h, pos):
            if isinstance(pos, int) and pos == 2:
                eng.wait_ge(pb_done[0], USES * h + 2)
            elif not isinstance(pos, int) or pos > 2:
                eng.wait_ge(pb_done[1], USES * h + pos - 1)
            elif h > 0:
                slot_free_c(eng, h - 1, TG, pos)

        def slot_free_c(eng, h, tg, e):
            if not isinstance(e, int) or e >= 2:
                eng.wait_ge(c_used, (TG * h + tg) * (C_STEPS - 1) + e - 1)
            elif tg == 0:
                eng.wait_ge(pb_done[1], USES * (h + 1) + e - 1)
            elif e == 0:
                eng.wait_ge(c_used, (TG * h + tg) * (C_STEPS - 1))
            else:
                eng.wait_ge(c_done, (TG * h + tg) * TPG)

        SMALL = 256

        def size_b(r):
            return SMALL if r >= 4 else 1024

        block = ctx.enter_context(nc.Block())

        @block.sync
        def _(sp):
            def load(b, slot, src, size=1024, slot_first=False):
                if not slot_first:
                    sp.wait_ge(w_lo, b - 1)
                sp.dma_start(wraw[:, slot, 0:size], src).then_inc(w_in[slot], 16)

            sp.dma_start(xr[:, 0, :], x[0, 0]).then_inc(x_first[0], 16)
            sp.dma_start(xr[:, 1, :], x[0, 1]).then_inc(x_first[1], 16)
            sp.dma_start(gainn[:, :], gain_n).then_inc(gn_first, 16)
            for t in range(2, 4):
                sp.dma_start(xr[:, t, :], x[0, t]).then_inc(x_first[t], 16)
            load(0, 0, wa[0], slot_first=True)
            load(1, 1, wa[1], slot_first=True)
            for h in range(HALVES):
                if h > 0:
                    for a in range(2):
                        load(block_a(h, a), a, wa[a])
                with sp.Fori(1, A_TILES // 2) as i:
                    for slot in range(2):
                        load(block_a(h, 2 * i + slot), slot, wa[2 * i + slot])
                with sp.Fori(0, NG) as g:
                    for r in range(4):
                        load(block_b(h, g, r), r % 2, wb[g, r])
                    for r in range(2):
                        load(block_b(h, g, 4 + r), r, wp[g, r], SMALL)
                for tg in range(TG):
                    with sp.Fori(0, C_STEPS // 2) as i:
                        for slot in range(2):
                            load(block_c(h, tg, 2 * i + slot), slot, wo[2 * i + slot])
            for t in range(TPG):
                sp.wait_ge(f_out, NTT * (HALVES - 1) + TPG + t + 1)
                sp.dma_start(out[HALVES - 1, TPG + t], rows[1][:, t, :]).then_inc(out_last, 16)
            sp.wait_ge(out_last, 16 * TPG)

        @block.gpsimd
        def _(pool):
            gp = nc.gpsimd
            gp.memset(kh[:, :, :].bitcast(F32), 0.0).then_inc(zero_r, 1)
            gp.dma_start(ident[:, :], ident_d).then_inc(ident_in, 16)
            gp.dma_start(cst[:, :], consts).then_inc(const_in, 16)
            gp.dma_start(rotm[:, :, :], rot_meta).then_inc(const_in, 16)
            gp.dma_start(meta_rows[:, :], meta).then_inc(meta_in, 16)
            gp.memset(kl[:, :, :].bitcast(F32), 0.0).then_inc(s_done, CREDIT)
            gp.memset(vh[:, :, :].bitcast(F32), 0.0).then_inc(o_gate, CREDIT)
            gp.memset(vl[:, :, :].bitcast(F32), 0.0).then_inc(o_done, CREDIT)

            def load_tables(h):
                gp.dma_start(cos_t[:, :], rot[h, 0]).then_inc(rot_tab, 16)
                gp.dma_start(sin_t[:, :], rot[h, 1]).then_inc(rot_tab, 16)

            def store_rows(h, tg):
                with pool.Fori(0, TPG) as t:
                    pool.wait_ge(f_out, NTT * h + TPG * tg + t + 1)
                    gp.dma_start(out[h, TPG * tg + t], rows[tg][:, t, :]).then_inc(out_done[tg], 16)

            for h in range(HALVES):
                for t in range(4, NTT):
                    pool.wait_ge(z_t, NTT * h + t - 4 + 1)
                    gp.dma_start(xr[:, t - 4, :], x[h, t]).then_inc(x_in[t - 4], 16)
                if h == 0:
                    load_tables(0)
                pool.wait_ge(rot_tab, 32 * (h + 1))
                if h == 0:
                    pool.wait_ge(const_in, 32)

                def times_cos(r):
                    settle(pool)
                    pool.wait_ge(rot_sw, r + 1)
                    gp.tensor_tensor(rotsrc[:, :], rotsrc[:, :], cos_t[:, :], ALU.mult).then_inc(rot_cos, 1)

                times_cos((1 + HT) * h)
                if h == 0:
                    pool.wait_ge(km_sw, 1)
                    gp.tensor_tensor(km[:, :], km[:, :], rotm[:, 0, :], ALU.mult).then_inc(km_chain, 1)
                    gp.tensor_tensor(kms[:, :], kms[:, :], rotm[:, 1, :], ALU.mult).then_inc(km_chain, 1)
                    pool.wait_ge(km_chain, 2)
                    gp.tensor_tensor(km[:, :], km[:, :], kms[:, :], ALU.add).then_inc(km_chain, 1)
                    pool.wait_ge(km_chain, 3)
                    pool.wait_ge(zero_r, 1)
                    pool.wait_ge(s_done, 1)
                    for kv in range(2):
                        gp.tensor_tensor(kmm[:, kv, :], km[:, :], cst[:, kv:kv + 1].to_broadcast([P, META]), ALU.mult).then_inc(km_chain, 1)
                    pool.wait_ge(km_chain, 5)
                    gp.tensor_copy(kh[:, 0, META0:KPITCH].rearrange("p (k t) -> p k t", t=META), kmm[:, :, :]).then_inc(km_chain, 1)
                    pool.wait_ge(km_chain, 6)
                    gp.tensor_tensor(kl[:, 0, META0:KPITCH].rearrange("p (k t) -> p k t", t=META), kmm[:, :, :],
                                     kh[:, 0, META0:KPITCH].bitcast(F32).rearrange("p (k t) -> p k t", t=META), ALU.subtract).then_inc(km_done, 1)
                    pool.wait_ge(m_ev, 2)
                    for kv in range(2):
                        last = gp.tensor_tensor(vmm[:, META * kv:META * kv + META], vm[:, :], cst[:, kv:kv + 1].to_broadcast([P, META]), ALU.mult)
                    last.then_inc(vmm_r, 1)
                if h > 0:
                    store_rows(h - 1, TG - 1)
                with pool.Fori(0, HT) as j:
                    times_cos((1 + HT) * h + 1 + j)
                pool.wait_ge(rot_done, (1 + HT) * (h + 1))
                gp.memset(ubuf[:, 0:PRE - META], 0.0).then_inc(u_halo, 1)

                with pool.Fori(0, NCH // 2) as pair:
                    for slot in range(2):
                        n = NCH * h + 2 * pair + slot
                        c = 2 * pair + slot
                        keys = slice(CH * slot, CH * slot + CH)
                        settle(pool)
                        pool.wait_ge(s_done, n + CREDIT)
                        gp.tensor_tensor(kmask[:, :, :], qk[:, c, 0:1, :].to_broadcast([P, 2, CH]),
                                         cst[:, 0:2].unsqueeze(2).to_broadcast([P, 2, CH]), ALU.mult).then_inc(ks_m, 1)
                        gp.tensor_copy(qh[:, :].rearrange("p (j t) -> p j t", t=CH), qk[:, c, 1:1 + HT, :]).then_inc(qs_hi, 1)
                        settle(pool)
                        pool.wait_ge(ks_m, n + 1)
                        gp.tensor_copy(kh[:, :, keys], kmask[:, :, :]).then_inc(ks_hi, 1)
                        settle(pool)
                        pool.wait_ge(qs_hi, n + 1)
                        gp.tensor_tensor(ql[:, :].rearrange("p (j t) -> p j t", t=CH), qk[:, c, 1:1 + HT, :],
                                         qh[:, :].bitcast(F32).rearrange("p (j t) -> p j t", t=CH), ALU.subtract).then_inc(qs_lo, 1)
                        settle(pool)
                        pool.wait_ge(ks_hi, n + 1)
                        gp.tensor_tensor(kl[:, :, keys], kmask[:, :, :], kh[:, :, keys].bitcast(F32), ALU.subtract).then_inc(qs_ready, 1)

                pool.wait_ge(pb_free[1], FREES * (h + 1) - 2 + CREDIT)
                pool.wait_ge(gs_hi, C_BLOCKS * h + 1)
                gp.tensor_tensor(gsl[:, 0, :], gates[:, 0, 0:TB], gsh[:, 0, :].bitcast(F32), ALU.subtract).then_inc(gs_first, 1)

                pool.wait_ge(vw_lo, NCH * (h + 1))
                pool.wait_ge(pb_done[1], USES * (h + 1))
                pool.wait_ge(o_done, NCH * (h + 1) + CREDIT)
                gp.dma_start(gainf[:, :], gain_f).then_inc(gf_in, 16)
                if h + 1 < HALVES:
                    gp.dma_start(gainn[:, :], gain_n).then_inc(gn_in, 16)
                    load_tables(h + 1)
                for tg in range(TG):
                    for t in range(TPG):
                        pool.wait_ge(c_used, (TG * h + tg) * (C_STEPS - 1) + 3 * t + 1)
                        gp.dma_start(rows_in[tg][:, t, :], x[h, TPG * tg + t]).then_inc(res_in, 16)
                        if tg == 0 and h + 1 < HALVES:
                            pool.wait_ge(c_used, (TG * h + tg) * (C_STEPS - 1) + 3 * t + 2)
                            gp.dma_start(xr[:, t, :], x[h + 1, t]).then_inc(x_in[t], 16)
                        if tg == 1:
                            pool.wait_ge(f_out, NTT * h + t + 1)
                            gp.dma_start(out[h, t], rows[0][:, t, :]).then_inc(out_done[0], 16)
                pool.wait_ge(c_used, (TG * h + 1) * (C_STEPS - 1) + HT + 1)
                gp.dma_start(gainf1[:, :], gain_f).then_inc(gf_in, 16)
            for tg in range(TG):
                pool.wait_ge(out_done[tg], 16 * TPG * (HALVES - tg))

        @block.scalar
        def _(act):
            sc = nc.scalar

            def split_hi(h, pos, slot, size=1024):
                if isinstance(pos, tuple):
                    b = block_c(h, *pos)
                    slot_free_c(act, h, *pos)
                else:
                    b = BLOCKS * h + pos
                    slot_free(act, h, pos)
                act.wait_ge(w_in[slot], 8 * (b - slot + 2))
                sc.activation(wh[:, slot, 0:size], wraw[:, slot, 0:size], ACT.Copy).then_inc(w_hi, 1)

            def square(src, junk, acc):
                return sc.activation(junk, src, ACT.Square, scale=1.0 / 32.0, accum_out=acc)

            def z_head(h, t):
                if h == 0 and t < 4:
                    act.wait_ge(x_first[t], 16)
                else:
                    act.wait_ge(x_in[t % 4], 16 * (2 * h + t // 4))
                square(xr[:, t % 4, :], junk[:, :], ssq[:, t % 4:t % 4 + 1]).then_inc(z_ssq, 1)
                act.wait_ge(z_ssq, NTT * h + t + 1)
                sc.activation(std[:, t % 4:t % 4 + 1], ssq[:, t % 4:t % 4 + 1], ACT.Sqrt, bias=epst).then_inc(z_std, 1)

            def z_tail(h, t):
                act.wait_ge(z_t, NTT * h + t + 1)
                sc.activation(zh[:, t, :, :].rearrange("p k t -> p (k t)"),
                              ps[:, z_bank(t):z_bank(t) + 2, :].rearrange("p b n -> p (b n)"), ACT.Copy).then_inc(z_hi, 1)

            def final_stats(h, t, spill=junk[:, :]):
                k = NTT * h + t
                act.wait_ge(h_add, k + 1)
                square(rows[t // TPG][:, t % TPG, :], spill, f_ss[:, t % 4:t % 4 + 1]).then_inc(f_ssq, 1)
                act.wait_ge(f_ssq, k + 1)
                sc.activation(f_sd[:, t % 4:t % 4 + 1], f_ss[:, t % 4:t % 4 + 1], ACT.Sqrt, bias=epst).then_inc(f_std, 1)

            def copy_meta(count):
                act.wait_ge(m_prod, count + 1)
                sc.activation(mprod[0:2 * META, :], ps[0:2 * META, SPARE, 0:2 * P], ACT.Copy).then_inc(m_sb, 1)

            for h in range(HALVES):
                if h == 0:
                    act.wait_ge(eps_r, 1)
                    sc.activation(f_sd[:, 3:4], epst, ACT.Sqrt)
                    z_head(0, 0)
                    z_head(0, 1)
                    z_head(0, 2)
                    z_tail(0, 0)
                    z_head(0, 3)
                    z_tail(0, 1)
                    split_hi(0, 0, 0)
                    z_tail(0, 2)
                    z_tail(0, 3)
                else:
                    for t in range(4):
                        z_tail(h, t)

                def to_rotary(h, a, r):
                    for tb in range(NTB):
                        act.wait_ge(pb_done[tb], use_a(h, a) + 1)
                        if tb == 0:
                            act.wait_ge(rot_done, r)
                        i = sc.activation(rotsrc[:, tb * TB:tb * TB + TB], ps[:, PB[tb], :], ACT.Copy)
                        i.then_inc(rot_in, 1)

                def copy_v(h, tb):
                    act.wait_ge(pb_done[1], use_a(h, 0) + tb + 1)
                    sc.activation(wsum[:, tb * TB:tb * TB + TB], ps[:, PB[1], :], ACT.Copy).then_inc(v_in, 1)

                def copy_k(h, tb):
                    act.wait_ge(pb_done[0], use_a(h, 0) + tb + 1)
                    sc.activation(rotsrc[:, tb * TB:tb * TB + TB], ps[:, (0, PB[0])[tb], :], ACT.Copy).then_inc(rot_in, 1)

                z_head(h, 4)
                z_head(h, 5)
                z_head(h, 6)
                split_hi(h, 1, 1)
                copy_k(h, 0)
                z_head(h, 7)
                if h == 0:
                    act.wait_ge(meta_in, 16)
                    square(meta_rows[:, :], junk[0:META, :], f_ss[0:META, 0:1]).then_inc(zm_step, 1)
                    act.wait_ge(zm_step, 1)
                    sc.activation(f_sd[0:META, 0:1], f_ss[0:META, 0:1], ACT.Sqrt, bias=epst[0:META]).then_inc(zm_step, 1)
                if h > 0:
                    act.wait_ge(out_done[0], 16 * TPG * h)
                for t in range(4, NTT):
                    z_tail(h, t)
                copy_v(h, 0)
                if h == 0:
                    act.wait_ge(zm_step, 5)
                    sc.activation(zm[:, :, 0, :], ps[:, SPARE, 0:KT * META].rearrange("p (k t) -> p k t", t=META), ACT.Copy).then_inc(zm_step, 1)
                copy_k(h, 1)
                if h == 0:
                    copy_meta(0)
                split_hi(h, 2, 0)
                copy_v(h, 1)
                if h == 0:
                    copy_meta(1)
                else:
                    act.wait_ge(z_lo, NTT * (h + 1))
                    for t in range(TPG, NTT):
                        final_stats(h - 1, t, ps[:, 2:4, :].rearrange("p b n -> p (b n)"))
                act.wait_ge(v_t, h + 1)
                sc.activation(vtok[:, :, :].rearrange("p m f -> p (m f)"), ps[:, 0:2, :].rearrange("p b n -> p (b n)"), ACT.Copy).then_inc(v_tok, 1)
                if h == 0:
                    act.wait_ge(vm_t, 1)
                    sc.activation(vmeta[0:32, :], ps[0:32, SPARE, 0:P], ACT.Copy)
                    sc.activation(vmeta[32:64, :], ps[0:32, SPARE, 0:P], ACT.Copy).then_inc(vm_hi, 1)

                def tanh(use, tb):
                    act.wait_ge(pb_done[tb], use + 1)
                    sc.activation(wsum[:, tb * TB:tb * TB + TB], ps[:, PB[tb], :], ACT.Tanh, scale=0.5).then_inc(tanh_r, 1)

                with act.Fori(0, HT) as j:
                    split_hi(h, 3 + 2 * j, 1)
                    to_rotary(h, 2 + 2 * j, (1 + HT) * h + 1 + j)
                    split_hi(h, 4 + 2 * j, 0)
                    for tb in range(NTB):
                        tanh(use_a(h, 3 + 2 * j), tb)

                with act.Fori(0, NG) as g:
                    for sub in range(4):
                        n = NCH * h + 4 * g + sub
                        split_hi(h, A_TILES + GROUP_BLOCKS * g + sub + 1, (sub + 1) % 2, size_b(sub + 1))
                        act.wait_ge(s_negm, n + 1)
                        for u in range(4):
                            for kv in range(2):
                                i = sc.activation(probs[:, u, kv * KEYS:kv * KEYS + KEYS], ps[:, u, kv * KEYS:kv * KEYS + KEYS], ACT.Exp,
                                                  bias=negm[:, 2 * u + kv:2 * u + kv + 1], scale=SCALE,
                                                  accum_out=den[:, 2 * u + kv:2 * u + kv + 1])
                            if u == 0:
                                act.wait_ge(s_sarg, n + 1)
                                sc.activation(esink, sarg, ACT.Exp)
                            elif u % 2 == 1:
                                i.then_inc(s_exp, 1)
                        if sub in (1, 2):
                            ut = PT * h + 2 * g + sub - 1
                            act.wait_ge(u_pool, ut + 1)
                            sc.activation(plh[:, sub - 1, :], wsum[:, META:META + TOK], ACT.Copy).then_inc(u_hi, 1)

                        def copy_out(tb):
                            if sub < 2:
                                act.wait_ge(pb_done[tb], use_b(h, g, sub) + 1)
                                if tb == 0:
                                    act.wait_ge(u_halo, (1 + PT) * h + 1 + 2 * g + sub + h)
                                sc.activation(ubuf[:, PRE + tb * TB:PRE + tb * TB + TB], ps[:, PB[tb], :], ACT.Copy).then_inc(u_in, 1)
                            else:
                                if sub == 2 and tb == 0:
                                    act.wait_ge(u_lo, PT * h + 2 * g + 2)
                                tanh(use_b(h, g, sub), tb)

                        copy_out(0)
                        if h == 0 and sub < 2:
                            copy_meta(2 + 2 * g + sub)
                        slot = sub % 2
                        lo_p, hi_p = slot * CH, slot * CH + CH
                        act.wait_ge(o_done, n + CREDIT)
                        sc.activation(vh[lo_p:hi_p, 0:4:3, :], vtok[lo_p:hi_p, 2 * g + sub // 2, :].rearrange("p (k d) -> p k d", k=2),
                                      ACT.Copy).then_inc(vw_hi, 1)
                        act.wait_ge(t_done, n + 1)
                        for kv in range(2):
                            sc.activation(pth[:, kv, :], ps[:, kv, :], ACT.Copy).then_inc(pt_hi, 1)
                        sc.activation(ptm[0:32, :], ps[0:32, 2, :], ACT.Copy).then_inc(pt_hi, 1)
                        sc.activation(ptm[64:96, :], ps[0:32, 2, :], ACT.Copy).then_inc(pt_hi, 1)
                        copy_out(1)
                    split_hi(h, A_TILES + GROUP_BLOCKS * g + 5, 1, SMALL)
                    split_hi(h, A_TILES + GROUP_BLOCKS * g + 6, 0)

                def gated_hi(tg, e, slot):
                    slot_free_c(act, h, tg, e)
                    sc.activation(gsh[:, slot, :], gates[:, e, tg * TB:tg * TB + TB], ACT.Copy).then_inc(gs_hi, 1)

                act.wait_ge(o_gate, NCH * h + NCH // TG + CREDIT)
                sc.activation(gsh[:, 0, :], gates[:, 0, 0:TB], ACT.Copy).then_inc(gs_hi, 1)
                act.wait_ge(o_gate, NCH * (h + 1) + CREDIT)
                act.wait_ge(pb_free[0], FREES * (h + 1) + CREDIT)
                act.wait_ge(pb_free[1], FREES * (h + 1) + CREDIT)
                for tg in range(TG):
                    last_group = h + 1 == HALVES and tg + 1 == TG

                    def step(e, slot):
                        split_hi(h, (tg, e + 1), 1 - slot)
                        gated_hi(tg, e + 1, 1 - slot)

                    peeled = 2 if tg == 0 else 8
                    for e in range(peeled):
                        step(e, e % 2)
                        if tg > 0 and e < 4:
                            final_stats(h, e)
                        elif tg > 0 and h + 1 < HALVES:
                            z_head(h + 1, e - 4)
                    with act.Fori(peeled // 2, C_STEPS // 2 - 1) as i:
                        step(2 * i, 0)
                        step(2 * i + 1, 1)
                    step(C_STEPS - 2, 0)
                    if tg + 1 < TG:
                        split_hi(h, (tg + 1, 0), 0)
                        gated_hi(tg + 1, 0, 0)
                    elif not last_group:
                        split_hi(h + 1, 0, 0)
            for t in range(TPG, NTT):
                final_stats(HALVES - 1, t)

        @block.vector
        def _(dve):
            ve = nc.vector

            def split_lo(b, slot, size=1024):
                dve.wait_ge(w_hi, b + 1)
                ve.tensor_tensor(wl[:, slot, 0:size], wraw[:, slot, 0:size], wh[:, slot, 0:size].bitcast(F32), ALU.subtract).then_inc(w_lo, 1)

            def hold():
                ve.memset(small[:, 13:14], 0.0)

            for tb in range(NTB):
                ve.memset(small[:, 14 + tb:15 + tb], 0.0).then_inc(pb_free[tb], CREDIT)
            ve.memset(epst, EPS).then_inc(eps_r, 1)

            def z_head(h, t):
                i = t % 4
                dve.wait_ge(z_std, NTT * h + t + 1)
                ve.reciprocal(rstd[:, i:i + 1], std[:, i:i + 1]).then_inc(z_rstd, 1)
                dve.wait_ge(z_rstd, NTT * h + t + 1)
                ve.scalar_tensor_tensor(xr[:, i, :], xr[:, i, :], rstd[:, i:i + 1], gainn[:, :], ALU.mult, ALU.mult).then_inc(z_norm, 1)

            def z_tail(h, t):
                dve.wait_ge(z_hi, NTT * h + t + 1)
                ve.tensor_tensor(zl[:, t, :, :].rearrange("p k t -> p (k t)"),
                                 ps[:, z_bank(t):z_bank(t) + 2, :].rearrange("p b n -> p (b n)"),
                                 zh[:, t, :, :].rearrange("p k t -> p (k t)").bitcast(F32), ALU.subtract).then_inc(z_lo, 1)

            def final_rows(h, t):
                k = NTT * h + t
                i = t % 4
                dve.wait_ge(f_std, k + 1)
                ve.reciprocal(f_rs[:, i:i + 1], f_sd[:, i:i + 1]).then_inc(f_rstd, 1)
                dve.wait_ge(f_rstd, k + 1)
                row = rows[t // TPG][:, t % TPG, :]
                gain = (gainf, gainf1)[t // TPG]
                if t == TPG:
                    dve.wait_ge(gf_in, 32 * (h + 1))
                ve.scalar_tensor_tensor(row, row, f_rs[:, i:i + 1], gain[:, :], ALU.mult, ALU.mult).then_inc(f_out, 1)

            dve.wait_ge(gn_first, 16)
            for t in range(4):
                z_head(0, t)
            z_tail(0, 0)
            z_tail(0, 1)
            split_lo(0, 0)
            z_tail(0, 2)
            z_tail(0, 3)

            for h in range(HALVES):
                if h > 0:
                    for t in range(4):
                        z_tail(h, t)

                SWAP = [(i + 8) % 16 if i < 16 else i for i in range(32)]

                def swap(r):
                    dve.wait_ge(rot_in, 2 * r + 2)
                    hold()
                    ve.stream_shuffle(swapped[:, :], rotsrc[:, :], SWAP).then_inc(rot_sw, 1)
                    dve.wait_ge(rot_sw, r + 1)
                    ve.tensor_tensor(swapped[:, :], swapped[:, :], sin_t[:, :], ALU.mult).then_inc(rot_sin, 1)

                def rotate(r, dst):
                    dve.wait_ge(rot_sin, r + 1)
                    dve.wait_ge(rot_cos, r + 1)
                    hold()
                    ve.tensor_tensor(dst, rotsrc[:, :].rearrange("p (c t) -> p c t", t=CH),
                                     swapped[:, :].rearrange("p (c t) -> p c t", t=CH), ALU.add).then_inc(rot_done, 1)

                def meta_sum(dst, count):
                    dve.wait_ge(m_done, count + 1)
                    ve.tensor_reduce(dst, ps[:, SPARE, 2 * P:2 * P + 2 * META].rearrange("p (l t) -> p t l", l=2), AXX, ALU.add).then_inc(m_ev, 1)

                def silu(dst, use, count, tb):
                    dve.wait_ge(tanh_r, count)
                    ve.scalar_tensor_tensor(dst, wsum[:, tb * TB:tb * TB + TB], 1.0, ps[:, PB[tb], :], ALU.add, ALU.mult).then_inc(pb_free[tb], 1)

                z_head(h, 4)
                z_head(h, 5)
                z_head(h, 6)
                split_lo(block_a(h, 1), 1)
                z_head(h, 7)
                for t in range(4, NTT):
                    z_tail(h, t)
                if h == 0:
                    dve.wait_ge(zm_step, 2)
                    ve.reciprocal(f_rs[0:META, 0:1], f_sd[0:META, 0:1]).then_inc(zm_step, 1)
                    dve.wait_ge(zm_step, 3)
                    ve.scalar_tensor_tensor(meta_rows[:, :], meta_rows[:, :], f_rs[0:META, 0:1], gainn[0:META, :], ALU.mult, ALU.mult).then_inc(zm_step, 1)
                    dve.wait_ge(const_in, 32)
                    ve.tensor_scalar(pgate, pscale, 0.5, None, ALU.mult).then_inc(psc_r, 1)
                    ve.tensor_scalar(nsinks, sinks, -1.0, None, ALU.mult).then_inc(psc_r, 1)
                    dve.wait_ge(psc_r, 2)
                if h == 0:
                    dve.wait_ge(zm_step, 6)
                    ve.tensor_tensor(zm[:, :, 1, :], ps[:, SPARE, 0:KT * META].rearrange("p (k t) -> p k t", t=META), zm[:, :, 0, :].bitcast(F32), ALU.subtract).then_inc(zm_step, 1)
                split_lo(block_a(h, 2), 0)
                dve.wait_ge(rot_tab, 32 * (h + 1))
                swap((1 + HT) * h)
                if h == 0:
                    meta_sum(km[:, :], 0)
                    dve.wait_ge(m_ev, 1)
                    ve.stream_shuffle(kms[:, :], km[:, :], SWAP).then_inc(km_sw, 1)
                rotate((1 + HT) * h, qk[:, :, 0, :])
                if h == 0:
                    meta_sum(vm[:, :], 1)
                else:
                    for t in range(TPG, NTT):
                        final_rows(h - 1, t)
                if h == 0:
                    dve.wait_ge(vm_hi, 1)
                    ve.tensor_tensor(vmeta[64:96, :], ps[0:32, SPARE, 0:P], vmeta[0:32, :].bitcast(F32), ALU.subtract).then_inc(vm_done, 1)
                with dve.Fori(0, HT) as j:
                    split_lo(block_a(h, 3 + 2 * j), 1)
                    swap((1 + HT) * h + 1 + j)
                    split_lo(block_a(h, 4 + 2 * j), 0)
                    rotate((1 + HT) * h + 1 + j, qk[:, :, 1 + j, :])
                    if h > 0:
                        dve.wait_ge(out_done[1], 16 * TPG * h)
                    for tb in range(NTB):
                        silu(gates[:, j, tb * TB:tb * TB + TB], use_a(h, 3 + 2 * j), (2 * HT + 2 * PT) * h + 2 * j + tb + 1, tb)

                with dve.Fori(0, NG) as g:
                    for sub in range(4):
                        n = NCH * h + 4 * g + sub
                        scores = ps[:, 0:4, 0:2 * KEYS].rearrange("p u (k s) -> p u k s", k=2)
                        dve.wait_ge(s_done, n + 1 + CREDIT)
                        if h == 0 and sub == 0:
                            for kv in range(2):
                                empty = ps[:, 0:4, kv * KPITCH + CH:kv * KPITCH + 2 * CH]
                                i = ve.tensor_scalar(empty, empty, cst[:, bass.ds(6 + g, 1)], None, ALU.add)
                                i.then_inc(s_mask, 1)
                            dve.wait_ge(s_mask, 2 * (g + 1))
                        ve.tensor_reduce(mx, scores, AXX, ALU.max).then_inc(s_max, 1)
                        dve.wait_ge(s_max, n + 1)
                        ve.scalar_tensor_tensor(negm, mx, -SCALE, nsinks, ALU.mult, ALU.min).then_inc(s_negm, 1)
                        dve.wait_ge(s_negm, n + 1)
                        ve.tensor_tensor(sarg, negm, sinks, ALU.add).then_inc(s_sarg, 1)
                        if sub in (1, 2):
                            ut = PT * h + 2 * g + sub - 1
                            dve.wait_ge(u_in, 2 * ut + 2)
                            if h == 0:
                                dve.wait_ge(m_ev, 2 + ut + 1)
                            hold()
                            ve.tensor_tensor_scan(wsum[:, :], ubuf[:, META:PRE + TOK], ubuf[:, bass.ds(META - (2 << g), META + TOK)], 0.0,
                                                  ALU.add, ALU.subtract).then_inc(u_sum, 1)
                            dve.wait_ge(u_sum, ut + 1)
                            ve.scalar_tensor_tensor(wsum[:, META:META + TOK], wsum[:, META:META + TOK], cst[:, bass.ds(2 + g, 1)],
                                                    ubuf[:, PRE:PRE + TOK], ALU.mult, ALU.subtract).then_inc(u_pool, 1)
                            if h == 0:
                                ve.tensor_copy(halo[:, 2 * g + sub - 1, :], ubuf[:, TOK + PRE - META:TOK + PRE]).then_inc(u_halo, 1)
                        if h > 0 and sub < 2:
                            dve.wait_ge(u_halo, 1 + PT + 1 + 2 * g + sub)
                            ve.tensor_copy(ubuf[:, PRE - META:PRE], halo[:, 2 * g + sub, :]).then_inc(u_halo, 1)
                        pr = probs[:, :, :].rearrange("p u (k s) -> p (u k) s", k=2)
                        for half in range(2):
                            heads = slice(4 * half, 4 * half + 4)
                            dve.wait_ge(s_exp, 2 * n + half + 1)
                            ve.tensor_tensor(dsum[:, heads], den[:, heads], esink[:, heads], ALU.add).then_inc(d_sum, 1)
                            dve.wait_ge(d_sum, 2 * n + half + 1)
                            ve.reciprocal(rden[:, heads], dsum[:, heads]).then_inc(d_rcp, 1)
                            dve.wait_ge(d_rcp, 2 * n + half + 1)
                            ve.tensor_tensor(pr[:, heads], pr[:, heads], rden[:, heads].unsqueeze(2).to_broadcast([P, 4, KEYS]), ALU.mult).then_inc(p_ready, 1)
                        if sub in (1, 2):
                            dve.wait_ge(u_hi, ut + 1)
                            ve.tensor_tensor(pll[:, sub - 1, :], wsum[:, META:META + TOK], plh[:, sub - 1, :].bitcast(F32), ALU.subtract).then_inc(u_lo, 1)
                        split_lo(block_b(h, g, sub + 1), (sub + 1) % 2, size_b(sub + 1))

                        def gate_tile(tb):
                            if sub >= 2:
                                silu(gates[:, HT + 2 * g + sub - 2, tb * TB:tb * TB + TB], None,
                                     (2 * HT + 2 * PT) * h + 2 * HT + 2 * (2 * g + sub - 2) + tb + 1, tb)

                        gate_tile(0)
                        slot = sub % 2
                        lo_p, hi_p = slot * CH, slot * CH + CH
                        dve.wait_ge(vw_hi, n + 1)
                        ve.tensor_tensor(vl[lo_p:hi_p, 0:4:3, :], vtok[lo_p:hi_p, 2 * g + sub // 2, :].rearrange("p (k d) -> p k d", k=2),
                                         vh[lo_p:hi_p, 0:4:3, :].bitcast(F32), ALU.subtract).then_inc(vw_lo, 1)
                        if h == 0 and sub < 2:
                            meta_sum(ubuf[:, PRE - META:PRE], 2 + 2 * g + sub)
                        for kv in range(2):
                            dve.wait_ge(pt_hi, 4 * n + kv + 1)
                            ve.tensor_tensor(ptl[:, kv, :], ps[:, kv, :], pth[:, kv, :].bitcast(F32), ALU.subtract)
                        dve.wait_ge(pt_hi, 4 * n + 4)
                        ve.tensor_tensor(ptm[32:64, :], ps[0:32, 2, :], ptm[0:32, :].bitcast(F32), ALU.subtract).then_inc(pt_lo, 1)
                        gate_tile(1)
                        dve.wait_ge(o_done, n + 1 + CREDIT)
                        gslice = gates[:, 0:HT, bass.ds((4 * g + sub) * CH, CH)]
                        ve.scalar_tensor_tensor(gslice, ps[:, OB, :].rearrange("p (j t) -> p j t", t=CH), 0.5, gslice, ALU.mult, ALU.mult).then_inc(o_gate, 1)
                    split_lo(block_b(h, g, 5), 1, SMALL)
                    for dt in range(2):
                        if dt == 1:
                            split_lo(block_b(h, g, 6), 0)
                        for tb in range(NTB):
                            dve.wait_ge(pb_done[tb], use_b(h, g, 4 + dt) + 1)
                            gt = gates[:, HT + 2 * g + dt, tb * TB:tb * TB + TB]
                            ve.scalar_tensor_tensor(gt, ps[:, PB[tb], :], stat[:, bass.ds(56 + 2 * g + dt, 1)], gt, ALU.mult, ALU.mult).then_inc(pb_free[tb], 1)

                def gated_lo(tg, e, slot):
                    b = C_BLOCKS * h + C_STEPS * tg + e
                    dve.wait_ge(gs_hi, b + 1)
                    ve.tensor_tensor(gsl[:, slot, :], gates[:, e, tg * TB:tg * TB + TB], gsh[:, slot, :].bitcast(F32), ALU.subtract).then_inc(gs_lo, 1)

                def add_rows(tg, t):
                    dve.wait_ge(c_done, NTT * h + tg * TPG + t + 1)
                    ve.tensor_tensor(rows[tg][:, t, :], ps[:, 2 * t:2 * t + 2, :].rearrange("p b n -> p (b n)"), rows_in[tg][:, t, :], ALU.add).then_inc(h_add, 1)

                for tg in range(TG):
                    last_group = h + 1 == HALVES and tg + 1 == TG

                    def step(e, slot):
                        split_lo(block_c(h, tg, e) + 1, 1 - slot)
                        gated_lo(tg, e + 1, 1 - slot)

                    peeled = 2 if tg == 0 else 8
                    for e in range(peeled):
                        step(e, e % 2)
                        if tg > 0 and e == 0:
                            dve.wait_ge(gf_in, 32 * h + 16)
                        if tg > 0 and e == 4 and h + 1 < HALVES:
                            dve.wait_ge(gn_in, 16 * (h + 1))
                        if tg > 0 and e < 4:
                            final_rows(h, e)
                        elif tg > 0 and h + 1 < HALVES:
                            z_head(h + 1, e - 4)
                    with dve.Fori(peeled // 2, C_STEPS // 2 - 1) as i:
                        step(2 * i, 0)
                        step(2 * i + 1, 1)
                    step(C_STEPS - 2, 0)
                    if not last_group:
                        split_lo(block_c(h, tg, C_STEPS - 1) + 1, 0)
                    if tg + 1 < TG:
                        gated_lo(tg + 1, 0, 0)
                    dve.wait_ge(res_in, 16 * (NTT * h + TPG * (tg + 1)))
                    for t in range(TPG):
                        add_rows(tg, t)
                        if last_group and t > 0:
                            final_rows(h, TPG + t - 1)
            final_rows(HALVES - 1, NTT - 1)

        @block.tensor
        def _(pe):
            te = nc.tensor

            def rhs_z(z, tb, k):
                return z[:, tb * (TB // P):(tb + 1) * (TB // P), k, :]

            def project_k0():
                pe.wait_ge(w_hi, block_a(h, 0) + 1)
                for pair in range(2):
                    cols = slice(2 * P * pair, 2 * P * (pair + 1))
                    pe.wait_ge(z_hi, NTT * h + 2 * pair + 2)
                    for k in range(KT):
                        te.matmul(ps[:, 0, cols], wh[:, 0, k * P:k * P + P], zh[:, 2 * pair:2 * pair + 2, k, :], start=pair == 0 and k == 0, stop=False)
                pe.wait_ge(w_lo, block_a(h, 0) + 1)
                for k in range(KT):
                    te.matmul(ps[:, 0, :], wl[:, 0, k * P:k * P + P], rhs_z(zh, 0, k), start=False, stop=False)
                pe.wait_ge(z_lo, NTT * h + 4)
                for k in range(KT):
                    last = te.matmul(ps[:, 0, :], wh[:, 0, k * P:k * P + P], rhs_z(zl, 0, k), start=False, stop=k == KT - 1)
                last.then_inc(pb_done[0], 1)

            def project(slot, tb, k0, k1, bank=None):
                bank = tb if bank is None else bank
                for k in range(k0, k1):
                    w_h, w_l = wh[:, slot, k * P:k * P + P], wl[:, slot, k * P:k * P + P]
                    te.matmul(ps[:, PB[bank], :], w_h, rhs_z(zh, tb, k), start=k == 0, stop=False)
                    te.matmul(ps[:, PB[bank], :], w_h, rhs_z(zl, tb, k), start=False, stop=False)
                    last = te.matmul(ps[:, PB[bank], :], w_l, rhs_z(zh, tb, k), start=False, stop=k == KT - 1)
                if k1 == KT:
                    last.then_inc(pb_done[bank], 1)
                return last

            def project_meta(slot):
                for k in range(KT):
                    last = te.matmul(ps[0:2 * META, SPARE, 0:2 * P], zm[:, k, :, :].rearrange("p l t -> p (l t)"),
                                     wsplit[:, slot, :, k * P:k * P + P], start=k == 0, stop=k == KT - 1)
                last.then_inc(m_prod, 1)

            def turn_meta(count):
                pe.wait_ge(m_sb, count + 1)
                for l in range(2):
                    last = te.matmul(ps[:, SPARE, 2 * P:2 * P + 2 * META], mprod[0:2 * META, l * P:l * P + P],
                                     ident[0:2 * META, 0:2 * META], start=l == 0, stop=l == 1)
                last.then_inc(m_done, 1)

            def z_transpose(h, t):
                pe.wait_ge(z_norm, NTT * h + t + 1)
                if t == 6:
                    pe.wait_ge(rot_in, 2 * (1 + HT) * h + 1)
                elif t > 3:
                    pe.wait_ge(z_lo, NTT * h + t - 2)
                elif h > 0:
                    pe.wait_ge(h_add, NTT * h - TPG + t + 1)
                for k in range(KT):
                    last = te.transpose(ps[:, z_bank(t) + k // 4, (k % 4) * P:(k % 4) * P + P], xr[:, t % 4, k * P:k * P + P], ident[:, :])
                last.then_inc(z_t, 1)

            pe.wait_ge(zero_r, 1)
            with pe.Fori(0, WARM // 4):
                for _ in range(4):
                    te.matmul(ps[:, SPARE, 0:2 * KEYS], kh[:, 0, 0:P], kh[:, :, :].rearrange("p k s -> p (k s)")[:, 0:2 * KEYS], start=True, stop=True)
            pe.wait_ge(ident_in, 16)
            for h in range(HALVES):
                for t in range(4):
                    z_transpose(h, t)
                if h > 0:
                    pe.wait_ge(h_add, NTT * h)

                def tile_a(a, slot, bank_free):
                    pe.wait_ge(w_lo, block_a(h, a) + 1)
                    for tb in range(NTB):
                        bank_free(tb)
                        project(slot, tb, 0, KT)

                pe.wait_ge(z_lo, NTT * h + 1)
                project_k0()
                for t in range(4, 7):
                    z_transpose(h, t)
                pe.wait_ge(w_lo, block_a(h, 1) + 1)
                project(1, 0, 0, 4, bank=1)
                z_transpose(h, 7)
                project(1, 0, 4, KT, bank=1)
                pe.wait_ge(z_lo, NTT * (h + 1))
                project(0, 1, 0, 4, bank=0)
                if h == 0:
                    pe.wait_ge(zm_step, 4)
                    for k in range(KT):
                        last = te.transpose(ps[:, SPARE, k * META:k * META + META], meta_rows[:, k * P:k * P + P], ident[0:META, 0:META])
                    last.then_inc(zm_step, 1)
                project(0, 1, 4, KT, bank=0)
                if h == 0:
                    pe.wait_ge(zm_step, 7)
                    project_meta(0)
                pe.wait_ge(v_in, 2 * h + 1)
                project(1, 1, 0, 4, bank=1)
                if h == 0:
                    turn_meta(0)
                project(1, 1, 4, KT, bank=1)
                if h == 0:
                    pe.wait_ge(m_ev, 1)
                    project_meta(1)

                pe.wait_ge(w_lo, block_a(h, 2) + 1)
                pe.wait_ge(rot_in, 2 * (1 + HT) * h + 2)
                project(0, 0, 0, 4)
                if h == 0:
                    turn_meta(1)
                project(0, 0, 4, KT)
                pe.wait_ge(v_in, 2 * (h + 1))
                for m in range(NTT):
                    last = te.transpose(ps[:, m // 4, (m % 4) * P:(m % 4) * P + P], wsum[:, m * P:m * P + P], ident[:, :])
                last.then_inc(v_t, 1)
                if h == 0:
                    pe.wait_ge(vmm_r, 1)
                    te.transpose(ps[0:32, SPARE, 0:P], vmm[:, :], ident[:, :]).then_inc(vm_t, 1)
                project(0, 1, 0, KT)

                def gate_tile(j):
                    tile_a(3 + 2 * j, 1, lambda tb: pe.wait_ge(rot_in, 2 * ((1 + HT) * h + 1 + j) + tb + 1))

                gate_tile(0)
                with pe.Fori(1, HT) as j:
                    tile_a(2 + 2 * j, 0, lambda tb: pe.wait_ge(pb_free[tb], FREES * h + j + CREDIT))
                    gate_tile(j)

                if h == 0:
                    pe.wait_ge(km_done, 1)
                    pe.wait_ge(vm_done, 1)
                with pe.Fori(0, NG) as g:
                    for sub in range(4):
                        n = NCH * h + 4 * g + sub
                        slot = sub % 2
                        pe.wait_ge(qs_ready, n + 1)
                        for u in range(4):
                            q_h, q_l = qh[:, u * P:u * P + P], ql[:, u * P:u * P + P]
                            so = ps[:, u, 0:2 * KEYS]
                            k_h, k_l = (w[:, :, :].rearrange("p k s -> p (k s)")[:, 0:2 * KEYS] for w in (kh, kl))
                            te.matmul(so, q_h, k_h, start=True, stop=False)
                            te.matmul(so, q_h, k_l, start=False, stop=False)
                            last = te.matmul(so, q_l, k_h, start=False, stop=True)
                        last.then_inc(s_done, 1)
                        pe.wait_ge(w_lo, block_b(h, g, sub) + 1)
                        ut = PT * h + 2 * g + sub

                        def bank_free(tb):
                            if sub in (1, 2):
                                pe.wait_ge(u_in, 2 * (ut - 1) + tb + 1)
                            else:
                                pe.wait_ge(pb_free[tb], FREES * h + HT + 4 * g + sub // 3 + CREDIT)

                        bank_free(0)
                        project(slot, 0, 0, KT)
                        if h == 0 and sub < 2:
                            pe.wait_ge(m_ev, 2 + 2 * g + sub)
                            project_meta(slot)
                        bank_free(1)
                        project(slot, 1, 0, SOFTMAX_STEPS)
                        for u in range(4):
                            if u % 2 == 0:
                                pe.wait_ge(p_ready, 2 * n + u // 2 + 1)
                            for kv in range(2):
                                te.transpose(ps[:, kv, u * P:u * P + P], probs[:, u, kv * KPITCH:kv * KPITCH + 2 * CH], ident[:, :])
                        for u in range(4):
                            last = te.transpose(ps[0:32, 2, u * P:u * P + P], probs[:, u, META0:KPITCH], ident[:, :])
                        last.then_inc(t_done, 1)
                        if h == 0 and sub < 2:
                            turn_meta(2 + 2 * g + sub)
                        project(slot, 1, SOFTMAX_STEPS, KT)
                        pe.wait_ge(pt_lo, n + 1)
                        pe.wait_ge(vw_lo, n + 1)
                        pe.wait_ge(o_gate, n + CREDIT)
                        ob = ps[:, OB, :]
                        for kv in range(2):
                            v_h = vh[:, 2 * kv:2 * kv + 2, :].rearrange("p a d -> p (a d)")
                            v_l = vl[:, 2 * kv:2 * kv + 2, :].rearrange("p a d -> p (a d)")
                            te.matmul(ob, v_h, pth[:, kv, :], start=kv == 0, stop=False)
                            te.matmul(ob, v_h, ptl[:, kv, :], start=False, stop=False)
                            te.matmul(ob, v_l, pth[:, kv, :], start=False, stop=False)
                        te.matmul(ob, vmeta[0:96, :], ptm[0:96, :], start=False, stop=True).then_inc(o_done, 1)
                    for dt in range(2):
                        pe.wait_ge(w_lo, block_b(h, g, 4 + dt) + 1)
                        pe.wait_ge(u_lo, PT * h + 2 * g + 2)
                        for tb in range(NTB):
                            pe.wait_ge(pb_free[tb], FREES * h + HT + 4 * g + 2 + dt + CREDIT)
                            mo = ps[:, PB[tb], :]
                            for ct in range(2):
                                m_h, m_l = wh[:, dt, ct * P:ct * P + P], wl[:, dt, ct * P:ct * P + P]
                                te.matmul(mo, m_h, plh[:, ct, tb * TB:tb * TB + TB], start=ct == 0, stop=False)
                                te.matmul(mo, m_h, pll[:, ct, tb * TB:tb * TB + TB], start=False, stop=False)
                                last = te.matmul(mo, m_l, plh[:, ct, tb * TB:tb * TB + TB], start=False, stop=ct == 1)
                            last.then_inc(pb_done[tb], 1)

                for tg in range(TG):
                    def step(e, slot, first=False, final=False, ts=range(TPG)):
                        pe.wait_ge(w_lo, block_c(h, tg, e) + 1)
                        if tg == 0 and first:
                            pe.wait_ge(gs_first, h + 1)
                        else:
                            pe.wait_ge(gs_lo, (C_BLOCKS - 1) * h + C_STEPS * tg + e)
                        for t in ts:
                            if first and tg > 0:
                                pe.wait_ge(h_add, NTT * h + (tg - 1) * TPG + t + 1)
                            elif first and t == OB // 2:
                                pe.wait_ge(o_gate, NCH * (h + 1) + CREDIT)
                            elif first and t == PB[0] // 2:
                                for tb in range(NTB):
                                    pe.wait_ge(pb_free[tb], FREES * (h + 1) + CREDIT)
                            g_h, g_l = gsh[:, slot, t * P:t * P + P], gsl[:, slot, t * P:t * P + P]
                            for dh in range(2):
                                w_h, w_l = wh[:, slot, dh * TB:dh * TB + TB], wl[:, slot, dh * TB:dh * TB + TB]
                                co = ps[:, 2 * t + dh, :]
                                te.matmul(co, g_h, w_h, start=first, stop=False)
                                te.matmul(co, g_h, w_l, start=False, stop=False)
                                last = te.matmul(co, g_l, w_h, start=False, stop=final)
                            if final:
                                last.then_inc(c_done, 1)
                        if not final:
                            last.then_inc(c_used, 1)

                    step(0, 0, first=True)
                    step(1, 1)
                    with pe.Fori(1, C_STEPS // 2 - 1) as i:
                        step(2 * i, 0)
                        step(2 * i + 1, 1)
                    if h + 1 < HALVES or tg + 1 < TG:
                        step(C_STEPS - 2, 0)
                        step(C_STEPS - 1, 1, final=True)
                    else:
                        for ts in ([0, 1], [2], [3]):
                            step(C_STEPS - 2, 0, ts=ts)
                            step(C_STEPS - 1, 1, final=True, ts=ts)


_INS = ["x", "meta", "wa", "wb", "wp", "wo", "gain_n", "gain_f", "consts", "ident", "rot", "rot_meta"]


def rotary_tables():
    half = HD // 4 // 2
    inv = (np.float32(500000.0) ** (-np.arange(half, dtype=np.float32) * np.float32(2.0 / (HD // 4)))).astype(np.float32)
    ang = np.arange(META + SEQ, dtype=np.float32)[None, :] * inv[:, None]
    cos, sin = np.cos(ang).astype(np.float32), np.sin(ang).astype(np.float32)
    c = np.ones((HD, META + SEQ), np.float32)
    s = np.zeros((HD, META + SEQ), np.float32)
    c[0:half], c[half:2 * half] = cos, cos
    s[0:half], s[half:2 * half] = -sin, sin
    return np.concatenate([c, c]), np.concatenate([s, s])


def kernel(x, meta_tokens, norm_gain, w_in, attn_sinks, w_pool, pool_scale, w_out, final_norm_gain):
    import concourse.bacc as bacc
    from concourse.bass_utils import run_bass_kernel_spmd

    w = np.asarray(w_in)[0]
    pairs = [np.r_[j * HD:(j + 1) * HD, (HT + j) * HD:(HT + j + 1) * HD] for j in range(HT)]
    q0, k0, v0, g0 = 0, HT * P, HT * P + P, HT * P + 2 * P
    u0 = g0 + HT * P
    p0 = u0 + PT * P

    def tiles(cols):
        t = w[:, np.stack(cols)]
        return np.ascontiguousarray(t.reshape(KT, P, len(cols), P).transpose(2, 1, 0, 3).reshape(len(cols), P, KT * P))

    cols = [np.arange(k0, k0 + P), np.arange(v0, v0 + P)]
    for j in range(HT):
        cols += [q0 + pairs[j], g0 + pairs[j]]
    wa = tiles(cols)
    cols = []
    for g in range(NG):
        for first in (u0, p0):
            cols += [np.arange(first + (2 * g + i) * P, first + (2 * g + i + 1) * P) for i in range(2)]
    wb = tiles(cols).reshape(NG, 4, P, KT * P)
    wp = np.ascontiguousarray(np.asarray(w_pool)[0].reshape(NG, 2, P, 2, P).transpose(0, 3, 2, 1, 4).reshape(NG, 2, P, 2 * P))
    rows = np.concatenate(pairs + [HT * P + np.arange(PT * P)])
    wo = np.ascontiguousarray(np.asarray(w_out)[0][rows].reshape(C_STEPS, P, D))

    consts = np.zeros((P, 32), np.float32)
    consts[:HD, 0] = 1.0
    consts[HD:, 1] = 1.0
    consts[:, 2:6] = [0.5, 0.25, 0.125, 0.0625]
    consts[:, 6] = -1e30
    sinks = np.asarray(attn_sinks)[0]
    for u in range(4):
        for kv in range(2):
            for i in range(2):
                consts[i * CH:(i + 1) * CH, 10 + 2 * u + kv] = sinks[kv * 8 + 2 * u + i]
    consts[:, 18:26] = np.asarray(pool_scale)[0].reshape(PT, P).T
    cos, sin = rotary_tables()
    rot = np.stack([np.stack([t[:, META + h * TOK:META + (h + 1) * TOK] for t in (cos, sin)]) for h in range(HALVES)])
    rot_meta = np.stack([cos[:, :META], sin[:, :META]], axis=1)

    arrays = {
        "x": np.asarray(x)[0].reshape(HALVES, NTT, P, D),
        "meta": np.asarray(meta_tokens),
        "wa": wa, "wb": wb, "wp": wp, "wo": wo,
        "gain_n": np.broadcast_to(np.asarray(norm_gain)[0], (P, D)),
        "gain_f": np.broadcast_to(np.asarray(final_norm_gain), (P, D)),
        "consts": consts, "ident": np.eye(P, dtype=np.float32), "rot": rot, "rot_meta": rot_meta,
    }
    nc = bacc.Bacc("TRN2", target_bir_lowering=False, num_devices=1)
    ins, args = {}, []
    for name in _INS:
        a = np.ascontiguousarray(arrays[name])
        ins[f"in_{name}"] = a
        args.append(nc.dram_tensor(f"in_{name}", a.shape, mybir.dt.from_np(a.dtype), kind="ExternalInput").ap())
    out = nc.dram_tensor("out_y", (HALVES, NTT, P, D), F32, kind="ExternalOutput").ap()
    build(nc, *args, out)
    r = run_bass_kernel_spmd(nc, [ins], core_ids=[0])
    return r.results[0]["out_y"].reshape(1, SEQ, D)
```
